# Optimizing a Trainium2 kernel written in Bass

```python
import jax, jax.numpy as jnp
from jax import lax
import numpy as np

D_MODEL = 2048
BATCH = 1
SEQ = 256
DEPTH = 1

GRID_W = 64
CTX_LEN = 256
N_MIXERS = 3
CHUNK = 64
EPS = 1e-6
GATE_CLIP = 30.0

FFN_HIDDEN = -(-8 * D_MODEL // (3 * 256)) * 256

HG_DK = 128
HG_HEADS = D_MODEL // HG_DK
HG_KEY_W = HG_HEADS * HG_DK
HG_DV = D_MODEL // HG_HEADS
HG_VAL_W = HG_HEADS * HG_DV

GLA_HEADS = 4
GLA_KEY_W = D_MODEL // 2
GLA_VAL_W = D_MODEL
GLA_DK = GLA_KEY_W // GLA_HEADS
GLA_DV = GLA_VAL_W // GLA_HEADS
GLA_GATE_RANK = 16
GLA_GATE_NORM = 16.0

DN_DK = 128
DN_DV = 128
DN_QK_HEADS = D_MODEL // 128
DN_V_HEADS = 2 * DN_QK_HEADS
DN_KEY_W = DN_QK_HEADS * DN_DK
DN_VAL_W = DN_V_HEADS * DN_DV
DN_QKV_W = 2 * DN_KEY_W + DN_VAL_W
CONV_K = 5

N_HG = (DEPTH + N_MIXERS - 1) // N_MIXERS
N_GLA = (DEPTH + N_MIXERS - 2) // N_MIXERS
N_DN = DEPTH // N_MIXERS

kernel_name = "hybrid_bidir_hgrn2_gla_deltanet_dit"

def _rms_norm(t, w):
    tf = t.astype(jnp.float32)
    y = tf * lax.rsqrt(jnp.mean(tf * tf, axis=-1, keepdims=True) + EPS)
    return (y * w.astype(jnp.float32)).astype(t.dtype)

def _modulate(t, shift, scale):
    return t * (1.0 + scale) + shift

def _l2norm(t):
    return t * lax.rsqrt(jnp.sum(t * t, axis=-1, keepdims=True) + EPS)

def _heads(t, n):
    return jnp.swapaxes(t.reshape(t.shape[:-1] + (n, t.shape[-1] // n)), -3, -2)

def _merge_heads(t):
    t = jnp.swapaxes(t, -3, -2)
    return t.reshape(t.shape[:-2] + (-1,))

def _two_way(fwd, bwd):
    return jnp.stack([fwd, jnp.flip(bwd, axis=-2)])

def _join_ways(o):
    return o[0] + jnp.flip(o[1], axis=-2)

def _split_chunks(t):
    t = t.reshape(t.shape[:-2] + (t.shape[-2] // CHUNK, CHUNK, t.shape[-1]))
    return jnp.moveaxis(t, -3, 0)

def _merge_chunks(t):
    t = jnp.moveaxis(t, 0, -3)
    return t.reshape(t.shape[:-3] + (-1, t.shape[-1]))

def _masked_exp(mask, rel):
    return jnp.where(mask, jnp.exp(jnp.where(mask, rel, 0.0)), 0.0)

def gla_chunk_scan(q, k, v, log_g, s0):
    tri = jnp.tril(jnp.ones((CHUNK, CHUNK), dtype=bool))[:, :, None]

    def step(s, blk):
        qc, kc, vc, gc = blk
        b = jnp.cumsum(gc, axis=-2)
        dec = _masked_exp(tri, b[..., :, None, :] - b[..., None, :, :])
        scores = jnp.einsum('...td,...sd,...tsd->...ts', qc, kc, dec)
        o = (jnp.einsum('...ts,...sv->...tv', scores, vc)
             + jnp.einsum('...td,...dv->...tv', qc * jnp.exp(b), s))
        b_end = b[..., -1, :]
        s_new = (jnp.exp(b_end)[..., :, None] * s
                 + jnp.einsum('...sd,...sv->...dv', kc * jnp.exp(b_end[..., None, :] - b), vc))
        return s_new, o

    s_fin, o = lax.scan(step, s0, tuple(_split_chunks(t) for t in (q, k, v, log_g)))
    return _merge_chunks(o), s_fin

def delta_chunk_scan(q, k, v, beta, log_a, s0):
    strict = jnp.tril(jnp.ones((CHUNK, CHUNK), dtype=bool), -1)
    incl = jnp.tril(jnp.ones((CHUNK, CHUNK), dtype=bool))
    eye = jnp.eye(CHUNK, dtype=jnp.float32)
    dv = v.shape[-1]

    def step(s, blk):
        qc, kc, vc, bc, gc = blk
        g = jnp.cumsum(gc[..., 0], axis=-1)
        rel = g[..., :, None] - g[..., None, :]
        dec_strict = _masked_exp(strict, rel)
        dec_incl = _masked_exp(incl, rel)
        lower = bc * jnp.einsum('...td,...sd->...ts', kc, kc) * dec_strict
        eg = jnp.exp(g)[..., None]
        rhs = jnp.concatenate([bc * vc, bc * eg * kc], axis=-1)
        sol = lax.linalg.triangular_solve(eye + lower, rhs, left_side=True, lower=True,
                                          unit_diagonal=True)
        w = sol[..., :dv] - jnp.einsum('...tk,...kv->...tv', sol[..., dv:], s)
        qk = jnp.einsum('...td,...sd->...ts', qc, kc) * dec_incl
        o = eg * jnp.einsum('...tk,...kv->...tv', qc, s) + jnp.einsum('...ts,...sv->...tv', qk, w)
        s_new = (jnp.exp(g[..., -1])[..., None, None] * s
                 + jnp.einsum('...sk,...sv->...kv', kc * jnp.exp(g[..., -1:] - g)[..., None], w))
        return s_new, o

    s_fin, o = lax.scan(step, s0, tuple(_split_chunks(t) for t in (q, k, v, beta, log_a)))
    return _merge_chunks(o), s_fin

def _gated_out(o, gate, o_norm, w_o):
    o = _merge_heads(_rms_norm(o, o_norm)).astype(gate.dtype)
    return (o * jax.nn.silu(gate)) @ w_o

def _short_conv(t, w, on_grid):
    b, n, ch = t.shape
    if on_grid:
        rows = n // GRID_W
        t = t.reshape(b * rows, GRID_W, ch)
    y = lax.conv_general_dilated(t, w.astype(t.dtype)[:, None, :], (1,),
                                 [(CONV_K // 2, CONV_K // 2)],
                                 dimension_numbers=('NWC', 'WIO', 'NWC'),
                                 feature_group_count=ch)
    return y.reshape(b, n, ch)

def hgrn2_mixer(a_ctx, a_lat, lb, w_in, w_f, o_norm, w_o, ctx_out):
    f32 = jnp.float32

    def prep(a):
        q, v, g = jnp.split(a @ w_in, [HG_KEY_W, HG_KEY_W + HG_VAL_W], axis=-1)
        z = jnp.einsum('bld,wdk->wblk', a, w_f).astype(f32)
        z = jnp.clip(z, -GATE_CLIP, GATE_CLIP)
        log_f = jax.nn.log_sigmoid(z) + jnp.log1p(lb * jnp.exp(-z))
        k = _heads((1.0 - lb) * jax.nn.sigmoid(-z), HG_HEADS)
        log_f = _heads(log_f, HG_HEADS)
        q = _heads(jax.nn.silu(q.astype(f32)), HG_HEADS) * (HG_DK ** -0.5)
        v = _heads(v.astype(f32), HG_HEADS)
        return (_two_way(q, q), _two_way(k[0], k[1]), _two_way(v, v),
                _two_way(log_f[0], log_f[1])), g

    in_c, g_c = prep(a_ctx)
    in_l, g_l = prep(a_lat)
    s0 = jnp.zeros((2, a_lat.shape[0], HG_HEADS, HG_DK, HG_DV), f32)
    o_c, s_c = gla_chunk_scan(*in_c, s0)
    o_l, _ = gla_chunk_scan(*in_l, s_c)
    y_lat = _gated_out(_join_ways(o_l), g_l, o_norm, w_o)
    y_ctx = _gated_out(_join_ways(o_c), g_c, o_norm, w_o) if ctx_out else None
    return y_ctx, y_lat

def gla_mixer(a_ctx, a_lat, w_in, w_g1, w_g2, b_g, o_norm, w_o, ctx_out):
    f32 = jnp.float32

    def prep(a):
        q, k, v, r = jnp.split(a @ w_in, [GLA_KEY_W, 2 * GLA_KEY_W, 2 * GLA_KEY_W + GLA_VAL_W],
                               axis=-1)
        low = jnp.einsum('bld,wdr->wblr', a, w_g1)
        gl = jnp.einsum('wblr,wrk->wblk', low, w_g2) + b_g[:, None, None, :]
        log_a = _heads(jax.nn.log_sigmoid(gl.astype(f32)) / GLA_GATE_NORM, GLA_HEADS)
        q = _heads(q.astype(f32), GLA_HEADS) * (GLA_DK ** -0.5)
        k = _heads(k.astype(f32), GLA_HEADS)
        v = _heads(v.astype(f32), GLA_HEADS)
        return (_two_way(q, q), _two_way(k, k), _two_way(v, v),
                _two_way(log_a[0], log_a[1])), r

    in_c, r_c = prep(a_ctx)
    in_l, r_l = prep(a_lat)
    s0 = jnp.zeros((2, a_lat.shape[0], GLA_HEADS, GLA_DK, GLA_DV), f32)
    o_c, s_c = gla_chunk_scan(*in_c, s0)
    o_l, _ = gla_chunk_scan(*in_l, s_c)
    y_lat = _gated_out(_join_ways(o_l), r_l, o_norm, w_o)
    y_ctx = _gated_out(_join_ways(o_c), r_c, o_norm, w_o) if ctx_out else None
    return y_ctx, y_lat

def gated_deltanet_mixer(a_ctx, a_lat, w_in, conv_w, w_b, w_a, a_log, dt_bias, o_norm, w_o,
                         ctx_out):
    f32 = jnp.float32
    rep = DN_V_HEADS // DN_QK_HEADS

    def prep(a, on_grid):
        qkv, z = jnp.split(a @ w_in, [DN_QKV_W], axis=-1)
        qkv = jax.nn.silu(_short_conv(qkv, conv_w, on_grid)).astype(f32)
        q, k, v = jnp.split(qkv, [DN_KEY_W, 2 * DN_KEY_W], axis=-1)
        q = jnp.repeat(_l2norm(_heads(q, DN_QK_HEADS)), rep, axis=-3) * (DN_DK ** -0.5)
        k = jnp.repeat(_l2norm(_heads(k, DN_QK_HEADS)), rep, axis=-3)
        v = _heads(v, DN_V_HEADS)
        beta = jax.nn.sigmoid(jnp.einsum('bld,wdh->wblh', a, w_b).astype(f32))
        dt = jax.nn.softplus(jnp.einsum('bld,wdh->wblh', a, w_a).astype(f32)
                             + dt_bias.astype(f32)[:, None, None, :])
        log_decay = -jnp.exp(a_log.astype(f32))[:, None, None, :] * dt
        beta = jnp.swapaxes(beta, -1, -2)[..., None]
        log_decay = jnp.swapaxes(log_decay, -1, -2)[..., None]
        return (_two_way(q, q), _two_way(k, k), _two_way(v, v),
                _two_way(beta[0], beta[1]), _two_way(log_decay[0], log_decay[1])), z

    in_c, z_c = prep(a_ctx, False)
    in_l, z_l = prep(a_lat, True)
    s0 = jnp.zeros((2, a_lat.shape[0], DN_V_HEADS, DN_DK, DN_DV), f32)
    o_c, s_c = delta_chunk_scan(*in_c, s0)
    o_l, _ = delta_chunk_scan(*in_l, s_c)
    y_lat = _gated_out(_join_ways(o_l), z_l, o_norm, w_o)
    y_ctx = _gated_out(_join_ways(o_c), z_c, o_norm, w_o) if ctx_out else None
    return y_ctx, y_lat

def _swiglu(t, w_gate, w_up, w_down):
    return (jax.nn.silu(t @ w_gate) * (t @ w_up)) @ w_down

def setup_inputs(seed: int = 0) -> dict:
    key = jax.random.key(seed)
    ks = iter(jax.random.split(key, 40))
    f32 = jnp.float32

    def nrm(shape, fan_in=1, scale=1.0):
        return jax.random.normal(next(ks), shape, f32) * (scale * fan_in ** -0.5)

    def gain(shape):
        return 1.0 + 0.02 * jax.random.normal(next(ks), shape, f32)

    dt = jnp.exp(jax.random.uniform(next(ks), (N_DN, 2, DN_V_HEADS), f32,
                                    minval=np.log(1e-3), maxval=np.log(1e-1)))
    return {
        "x": nrm((BATCH, SEQ, D_MODEL)),
        "c": nrm((BATCH, D_MODEL)),
        "ctx": nrm((BATCH, CTX_LEN, D_MODEL)),
        "c_ctx": nrm((D_MODEL,)),
        "w_ada": nrm((DEPTH, D_MODEL, 6 * D_MODEL), D_MODEL, 0.5),
        "b_ada": nrm((DEPTH, 6 * D_MODEL), 1, 0.01),
        "norm_mix": gain((DEPTH, D_MODEL)),
        "norm_ffn": gain((DEPTH, D_MODEL)),
        "hg_lb_logits": nrm((DEPTH, HG_KEY_W), 1, 0.5),
        "hg_w_in": nrm((N_HG, D_MODEL, HG_KEY_W + 2 * HG_VAL_W), D_MODEL),
        "hg_w_f": nrm((N_HG, 2, D_MODEL, HG_KEY_W), D_MODEL),
        "hg_o_norm": gain((N_HG, HG_DV)),
        "hg_w_o": nrm((N_HG, HG_VAL_W, D_MODEL), HG_VAL_W),
        "gla_w_in": nrm((N_GLA, D_MODEL, 2 * GLA_KEY_W + 2 * GLA_VAL_W), D_MODEL),
        "gla_w_g1": nrm((N_GLA, 2, D_MODEL, GLA_GATE_RANK), D_MODEL),
        "gla_w_g2": nrm((N_GLA, 2, GLA_GATE_RANK, GLA_KEY_W), GLA_GATE_RANK),
        "gla_b_g": nrm((N_GLA, 2, GLA_KEY_W), 1, 0.1),
        "gla_o_norm": gain((N_GLA, GLA_DV)),
        "gla_w_o": nrm((N_GLA, GLA_VAL_W, D_MODEL), GLA_VAL_W),
        "dn_w_in": nrm((N_DN, D_MODEL, DN_QKV_W + DN_VAL_W), D_MODEL),
        "dn_conv": nrm((N_DN, CONV_K, DN_QKV_W), CONV_K),
        "dn_w_b": nrm((N_DN, 2, D_MODEL, DN_V_HEADS), D_MODEL),
        "dn_w_a": nrm((N_DN, 2, D_MODEL, DN_V_HEADS), D_MODEL),
        "dn_a_log": jnp.log(jax.random.uniform(next(ks), (N_DN, 2, DN_V_HEADS), f32,
                                               minval=1.0, maxval=16.0)),
        "dn_dt_bias": dt + jnp.log(-jnp.expm1(-dt)),
        "dn_o_norm": gain((N_DN, DN_DV)),
        "dn_w_o": nrm((N_DN, DN_VAL_W, D_MODEL), DN_VAL_W),
        "ffn_w_gate": nrm((DEPTH, D_MODEL, FFN_HIDDEN), D_MODEL),
        "ffn_w_up": nrm((DEPTH, D_MODEL, FFN_HIDDEN), D_MODEL),
        "ffn_w_down": nrm((DEPTH, FFN_HIDDEN, D_MODEL), FFN_HIDDEN),
        "final_norm": gain((D_MODEL,)),
    }

def reference(x, c, ctx, c_ctx, w_ada, b_ada, norm_mix, norm_ffn, hg_lb_logits, hg_w_in, hg_w_f,
              hg_o_norm, hg_w_o, gla_w_in, gla_w_g1, gla_w_g2, gla_b_g, gla_o_norm, gla_w_o,
              dn_w_in, dn_conv, dn_w_b, dn_w_a, dn_a_log, dn_dt_bias, dn_o_norm, dn_w_o,
              ffn_w_gate, ffn_w_up, ffn_w_down, final_norm):
    p = jax.nn.softmax(hg_lb_logits.astype(jnp.float32), axis=0)
    lower_bounds = jnp.cumsum(p, axis=0) - p[0]

    s_lat = jax.nn.silu(c)[:, None, :]
    s_ctx = jax.nn.silu(c_ctx)
    h_lat, h_ctx = x, ctx
    for i in range(DEPTH):
        keep_ctx = i < DEPTH - 1
        m_lat = jnp.split(s_lat @ w_ada[i] + b_ada[i], 6, axis=-1)
        m_ctx = jnp.split(s_ctx @ w_ada[i] + b_ada[i], 6, axis=-1)
        a_lat = _modulate(_rms_norm(h_lat, norm_mix[i]), m_lat[0], m_lat[1])
        a_ctx = _modulate(_rms_norm(h_ctx, norm_mix[i]), m_ctx[0], m_ctx[1])
        kind, j = i % N_MIXERS, i // N_MIXERS
        if kind == 0:
            y_ctx, y_lat = hgrn2_mixer(a_ctx, a_lat, lower_bounds[i], hg_w_in[j], hg_w_f[j],
                                       hg_o_norm[j], hg_w_o[j], keep_ctx)
        elif kind == 1:
            y_ctx, y_lat = gla_mixer(a_ctx, a_lat, gla_w_in[j], gla_w_g1[j], gla_w_g2[j],
                                     gla_b_g[j], gla_o_norm[j], gla_w_o[j], keep_ctx)
        else:
            y_ctx, y_lat = gated_deltanet_mixer(a_ctx, a_lat, dn_w_in[j], dn_conv[j], dn_w_b[j],
                                                dn_w_a[j], dn_a_log[j], dn_dt_bias[j],
                                                dn_o_norm[j], dn_w_o[j], keep_ctx)
        h_lat = h_lat + m_lat[2] * y_lat
        h_lat = h_lat + m_lat[5] * _swiglu(
            _modulate(_rms_norm(h_lat, norm_ffn[i]), m_lat[3], m_lat[4]),
            ffn_w_gate[i], ffn_w_up[i], ffn_w_down[i])
        if keep_ctx:
            h_ctx = h_ctx + m_ctx[2] * y_ctx
            h_ctx = h_ctx + m_ctx[5] * _swiglu(
                _modulate(_rms_norm(h_ctx, norm_ffn[i]), m_ctx[3], m_ctx[4]),
                ffn_w_gate[i], ffn_w_up[i], ffn_w_down[i])
    return _rms_norm(h_lat, final_norm)


_drawn_inputs = setup_inputs


def setup_inputs(seed=0):
    import zlib

    import numpy as np

    out = dict(_drawn_inputs(seed))
    spreads = {}
    factors = {'ctx': 8.0,
     'c_ctx': 8.0,
     'b_ada': 4.989,
     'norm_mix': 8.0,
     'norm_ffn': 21.368,
     'hg_w_f': 3.543,
     'hg_o_norm': 8.0,
     'final_norm': 7.656}
    for name, (base, spread) in spreads.items():
        noise = np.random.default_rng([zlib.crc32(name.encode()), seed]).standard_normal(out[name].shape)
        drawn = base * np.exp(spread * noise) if base else spread * noise
        out[name] = __import__('jax').numpy.asarray(drawn.astype(out[name].dtype))
    for name, factor in factors.items():
        out[name] = (out[name] * factor).astype(out[name].dtype)
    return out
```

```python
from contextlib import ExitStack

import numpy as np

import concourse.bass as bass
from concourse import mybir

F32 = mybir.dt.float32
F32R = mybir.dt.float32r
U32 = mybir.dt.uint32
ALU = mybir.AluOpType
ACT = mybir.ActivationFunctionType
EXP_LN = "natural_log_exp_and_others"

P = 128
D = 2048
T = 256
TT = 2 * T
KD = D // P
HEADS = 16
PAIRS = HEADS // 2
GROUPS = PAIRS // 2
HALVES = [64, 32, 16, 8, 4, 2, 1]
NL = len(HALVES)
FF = 5632
KF = FF // P
FG = FF // 512
EPS = 1e-6
CLIP = 30.0
QSCALE = float(P) ** -0.5

CW = 1024
RAW = 4
SPL = 2
BODY = 32
C_G = GROUPS * BODY
C_WO = C_G + 4 * 8
C_FF = C_WO + KD * 2
C_DN = C_FF + FG * 16
CHUNKS = C_DN + KF * 2
ADA0 = KD * 4
PADA = 8 * KD

R_NMIX, R_NFFN, R_FIN, R_LB, R_C, R_CCTX, R_ONORM = 0, 16, 32, 48, 64, 80, 96
VROWS = 97


def head_slots():
    return [(-5, -3), (3, -2), (11, -1), (19, 0), (27, 1)]


def tasks_at(p, groups=True):
    return [(p - s, off) for s, off in head_slots() if 0 <= p - s <= 10]


def tasks_tail(p):
    out = []
    for s, head, stretched in ((-5, HEADS - 3, False), (3, HEADS - 2, True), (15, HEADS - 1, True)):
        for j in range(11):
            at = s + (3 * j) // 2 if stretched else s + j
            if at == p:
                out.append((j, head))
    return out


def positions():
    for g in range(GROUPS):
        for p in range(BODY):
            kind = "Z" if p % 16 >= 8 else "VQ"
            tasks = [(j, 4 * g + off) for j, off in tasks_at(p) if 4 * g + off >= 0]
            yield g * BODY + p, kind, 2 * g + p // 16, p % 8, tasks
    for p in range(32):
        yield C_G + p, "G", p // 8, p % 8, tasks_tail(p)


def build(nc, x, c, ctx, c_ctx, w_ada, b_ada, norm_mix, norm_ffn, lb_logits, w_in, w_f, o_norm, w_o,
          w_gate, w_up, w_down, final_norm, ident_in, keep_in, masks_in, out):
    xrows = x.rearrange("b (t p) d -> (b t) p d", p=P)
    crows = ctx.rearrange("b (t p) d -> (b t) p d", p=P)
    orows = out.rearrange("b (t p) d -> (b t) p d", p=P)
    wada = w_ada[0].rearrange("(k p) n -> k p n", p=P)
    win = w_in[0].rearrange("(k p) n -> p k n", p=P)
    wf = [w_f[0, d].rearrange("(k p) n -> p k n", p=P) for d in range(2)]
    wo = w_o[0].rearrange("(k p) n -> k p n", p=P)
    wgu = [w[0].rearrange("(k p) n -> p k n", p=P) for w in (w_gate, w_up)]
    wdn = w_down[0].rearrange("(k p) n -> k p n", p=P)

    stack = ExitStack()
    with stack:
        def sb(name, shape, dt=F32):
            return stack.enter_context(nc.sbuf_tensor(name, shape, dt))

        def sem(name):
            return stack.enter_context(nc.semaphore(name))

        raw = sb("raw", [P, RAW, CW])
        whi = sb("whi", [P, SPL, CW], F32R)
        wlo = sb("wlo", [P, SPL, CW], F32R)
        ahi = sb("ahi", [P, KD, TT], F32R)
        alo = sb("alo", [P, KD, TT], F32R)
        arena = sb("arena", [P, 2 * 6144])
        xin = arena[:, 0:4 * D].rearrange("p (t d) -> p t d", t=4)
        h1 = arena[:, 0:KF * T].rearrange("p (k t) -> p k t", k=KF)
        outb = arena[:, 0:2 * D].rearrange("p (t d) -> p t d", t=2)
        pair = [arena[:, b * 6144:(b + 1) * 6144] for b in range(2)]
        gates = [a[:, 0:2048].rearrange("p (h d t) -> p h d t", h=2, d=2) for a in pair]
        keyq = [a[:, 2048:5120].rearrange("p (h s t) -> p h s t", h=2, s=3) for a in pair]
        vals = [a[:, 5120:6144].rearrange("p (t v) -> p t v", t=4) for a in pair]
        work = sb("work", [P, 4096 + 7680])
        oT = work[:, 0:4096].rearrange("p (k t) -> p k t", k=KD)
        hT = oT
        xT = work[:, 0:KD * TT].rearrange("p (k t) -> p k t", k=KD)
        ebuf = work[:, 4096:4096 + 3584].rearrange("p (d l t) -> p d l t", d=2, l=NL)
        eseq = work[:, 4096:4096 + 3584].rearrange("p (d n) -> p d n", d=2)
        pcum = work[:, 7680:8704].rearrange("p (d t) -> p d t", d=2)
        xs = work[:, 8704:9472].rearrange("p (d j t) -> p d j t", d=2, j=3)
        xi = work[:, 9472:9984].rearrange("p (d t) -> p d t", d=2)
        kt = work[:, 9984:10752].rearrange("p (d j t) -> p d j t", d=2, j=3)
        state = work[:, 10752:11264].rearrange("p (o d v) -> p o d v", o=2, d=2)
        pT = work[:, 11264:11520].rearrange("p (t n) -> p t n", t=2)
        ksum = work[:, 11520:11776]
        xres = work[:, 4096:8192].rearrange("p (k t) -> p k t", k=KD)

        rstd = sb("rstd", [P, TT])
        zt = sb("zt", [P, 2, 2, TT])
        sq = zt[:, :, 0, :]
        osq = rstd[:, T:TT]
        aw = sb("aw", [P, 2, CW])
        aacc = sb("aacc", [P, CW])
        yhi = ahi[:, 0:2, T:TT]
        ylo = alo[:, 0:2, T:TT]
        ident = sb("ident", [P, P])
        ones = sb("ones", [P, P])
        keep = sb("keep", [P, TT])
        masks = sb("masks", [P, 2 * NL * 64], U32)
        vrow = arena[:, 4 * D:4 * D + P]
        brow = arena[:, 4 * D + P:4 * D + 2 * P]
        vec = sb("vec", [P, VROWS])
        bias = sb("bias", [P, 96])
        eps = sb("eps", [P, 1])
        cs = sb("cs", [P, KD, 2])
        mod = sb("mod", [P, 6, KD])
        modc = sb("modc", [P, 2, KD])
        scl = sb("scl", [P, 2, KD])
        sclf = sb("sclf", [P, KD])
        lbt = sb("lbt", [P, 4, KD])
        lbv = lbt[:, 3, :]
        oml = sb("oml", [P, KD])
        tot = sb("tot", [P, 2, 2, 8])
        etot = sb("etot", [P, 2, 2])
        rcol = sb("rcol", [P, 2, 2])
        xdram = nc.dram_tensor("x_features", [P, KD * T], F32, kind="Internal").ap()

        bank = [stack.enter_context(nc.psum_tensor(f"bank{i}", [P, 512], F32)) for i in range(4)]
        score = stack.enter_context(nc.psum_tensor("score", [P, 2, 512], F32))
        mx = stack.enter_context(nc.psum_tensor("mx", [P, 512], F32))
        ob = stack.enter_context(nc.psum_tensor("ob", [P, 512], F32))
        all8 = [b[:, :] for b in bank] + [score[:, 0, :], score[:, 1, :], mx[:, :], ob[:, :]]

        s_const = sem("const_in")
        s_x = [sem(f"x_in{t}") for t in range(4)]
        s_vecT = sem("vectors_turned")
        s_vec = sem("vectors_ready")
        s_one = sem("ones_ready")
        s_cs = sem("silu_c_ready")
        s_lb = sem("lower_bound_steps")
        s_ada_in = [sem(f"ada_in{i}") for i in range(RAW)]
        s_ada_used = sem("ada_used")
        s_xt = sem("x_turned")
        s_xe = sem("x_evacuated")
        s_sq = sem("x_squared")
        s_ms = sem("x_mean_square")
        s_rs = sem("x_rstd")
        s_xs = sem("x_stored")
        s_xn = sem("x_normed")
        s_mod = sem("mod_steps")
        s_a = sem("a_value")
        s_ah = sem("a_hi")
        s_al = sem("a_lo")
        s_raw = [sem(f"raw_in{i}") for i in range(RAW)]
        s_hi = sem("hi_ready")
        s_lo = sem("lo_ready")
        s_used = sem("chunk_used")
        s_aw = [sem(f"aw_in{i}") for i in range(2)]
        s_az = sem("ada_cleared")
        s_am = sem("ada_products")
        s_ac = sem("ada_accumulated")
        s_ap = sem("ada_summed")
        s_av = sem("ada_evacuated")
        s_vev = sem("v_evacuated")
        s_qev = sem("q_evacuated")
        s_qs = sem("q_scaled")
        s_zc = sem("z_clipped")
        s_ze = sem("z_exps")
        s_zy = sem("z_log_f")
        s_zk = sem("z_sigmoid")
        s_k = sem("keys_ready")
        s_cd = sem("cumulated")
        s_cum = sem("totals_ready")
        s_sub = sem("exponents")
        s_ex = sem("state_exps")
        s_el = sem("level_exps")
        s_xm = sem("state_operands")
        s_em = sem("level_operands")
        s_tr = sem("keys_turned")
        s_kt = sem("turned_keys_ready")
        s_st = sem("states_summed")
        s_s1 = sem("first_state_ready")
        s_s2 = sem("second_state_ready")
        s_sc = sem("scores_ready")
        s_dg = sem("diagonal_placed")
        s_pl = sem("scores_placed")
        s_o = sem("outputs_ready")
        s_osq = sem("outputs_squared")
        s_om = sem("outputs_mean_square")
        s_ol = sem("outputs_ln")
        s_or = sem("outputs_rstd")
        s_on = sem("outputs_normed")
        s_gev = sem("gate_evacuated")
        s_y = sem("y_gated")
        s_yh = sem("y_hi")
        s_yl = sem("y_lo")
        s_wo = sem("wo_summed")
        s_xb = sem("x_back")
        s_h = sem("h_ready")
        s_hq = sem("h_squared")
        s_hm = sem("h_mean_square")
        s_hr = sem("h_rstd")
        s_ht = sem("h_scaled")
        s_fa = sem("ffn_in")
        s_fg = sem("ffn_gate")
        s_fgs = sem("ffn_gate_silu")
        s_fh = sem("ffn_hidden")
        s_dn = sem("down_summed")
        s_fo = sem("final_h")
        s_fq = sem("final_squared")
        s_fm = sem("final_mean_square")
        s_fr = sem("final_rstd")
        s_fs = sem("final_scaled")
        s_ft = sem("final_turned")
        s_fe = sem("final_evacuated")
        s_out = sem("out_stored")

        block = stack.enter_context(nc.Block())

        def unit_of(ck):
            return (ck - C_FF) // 8

        @block.sync
        def _(sp):
            for dst, src in ((ident, ident_in), (keep, keep_in), (masks, masks_in)):
                sp.dma_start(dst[:, :], src).then_inc(s_const, 16)
            rows = ((R_NMIX, norm_mix[0]), (R_NFFN, norm_ffn[0]), (R_FIN, final_norm), (R_LB, lb_logits[0]),
                    (R_C, c[0]), (R_CCTX, c_ctx))
            for r, v in rows:
                sp.dma_start(vrow[r:r + KD, :], v.rearrange("(k p) -> k p", p=P)).then_inc(s_const, 16)
            sp.dma_start(vrow[R_ONORM:R_ONORM + 1, :], o_norm).then_inc(s_const, 16)
            sp.dma_start(brow[0:96, :], b_ada[0].rearrange("(k p) -> k p", p=P)).then_inc(s_const, 16)
            for t in range(4):
                src = crows[t] if t < 2 else xrows[t - 2]
                sp.dma_start(xin[:, t, :], src).then_inc(s_x[t], 16)
            for i in range(ADA0):
                if i >= RAW:
                    sp.wait_ge(s_ada_used, i - RAW + 1)
                if i == RAW:
                    sp.wait_ge(s_xe, KD)
                    sp.dma_start(xdram.rearrange("p (k t) -> p k t", k=KD), xT[:, :, T:TT]).then_inc(s_xs, 16)
                k, q = divmod(i, 4)
                sp.dma_start(raw[:, i % RAW, :], wada[k, :, q * CW:(q + 1) * CW]).then_inc(s_ada_in[i % RAW], 16)

            def two(slot, dst, src):
                sp.dma_start(dst[0:64], src[0:64]).then_inc(s_raw[slot], 16)
                sp.dma_start(dst[64:P], src[64:P]).then_inc(s_raw[slot], 16)

            def load(ck):
                if ck < RAW:
                    sp.wait_ge(s_ada_used, ADA0 - RAW + ck + 1)
                else:
                    sp.wait_ge(s_lo, ck - RAW + 1)
                slot = ck % RAW
                dst = raw[:, slot, :]
                if ck < C_G:
                    pr, r = divmod(ck, 16)
                    kk = 2 * (r % 8)
                    a, b = (win, win) if r < 8 else (wf[0], wf[1])
                    ca = (D if r < 8 else 0) + pr * 256
                    cb = pr * 256
                    d3 = dst.rearrange("p (k n) -> p k n", k=2)
                    sp.dma_start(d3[:, :, 0:256], a[:, kk:kk + 2, ca:ca + 256]).then_inc(s_raw[slot], 16)
                    sp.dma_start(d3[:, :, 256:512], b[:, kk:kk + 2, cb:cb + 256]).then_inc(s_raw[slot], 16)
                elif ck < C_WO:
                    u, r = divmod(ck - C_G, 8)
                    d3 = dst.rearrange("p (k n) -> p k n", k=2)
                    col = 2 * D + u * 512
                    two(slot, d3, win[:, 2 * r:2 * r + 2, col:col + 512])
                elif ck < C_FF:
                    k, half = divmod(ck - C_WO, 2)
                    two(slot, dst, wo[k, :, half * CW:(half + 1) * CW])
                elif ck < C_DN:
                    u, r = divmod(ck - C_FF, 8)
                    d3 = dst.rearrange("p (k n) -> p k n", k=2)
                    two(slot, d3, wgu[u % 2][:, 2 * r:2 * r + 2, (u // 2) * 512:(u // 2) * 512 + 512])
                else:
                    k, half = divmod(ck - C_DN, 2)
                    two(slot, dst, wdn[k, :, half * CW:(half + 1) * CW])

            for ck in range(CHUNKS):
                load(ck)
                if ck < PADA:
                    if ck >= 2:
                        sp.wait_ge(s_ac, ck - 1)
                    e, k = divmod(ck, KD)
                    sp.dma_start(aw[:, ck % 2, :], wada[k, :, 2 * D + e * CW:2 * D + (e + 1) * CW]).then_inc(s_aw[ck % 2], 16)
                if ck == C_WO:
                    sp.wait_ge(s_on, HEADS)
                    sp.wait_ge(s_xs, 16)
                    sp.dma_start(xres, xdram.rearrange("p (k t) -> p k t", k=KD)).then_inc(s_xb, 16)
            for t in range(2):
                sp.wait_ge(s_fe, 4 * (t + 1))
                sp.dma_start(orows[t], outb[:, t, :]).then_inc(s_out, 16)
            sp.wait_ge(s_out, 32)

        @block.gpsimd
        def _(pool):
            for e in range(8):
                if e:
                    pool.wait_ge(s_ap, e)
                for k in range(KD):
                    i = e * KD + k
                    if k == 0:
                        pool.memset(aacc[:, :], 0.0).then_inc(s_az, 1)
                        pool.wait_ge(s_az, e + 1)
                    else:
                        pool.wait_ge(s_ac, i)
                    pool.wait_ge(s_am, i + 1)
                    pool.tensor_tensor(aacc[:, :], aw[:, i % 2, :], aacc[:, :], ALU.add).then_inc(s_ac, 1)

        def halves(ap, h):
            v = ap.rearrange("p d (b n) -> p d b n", n=2 * h)
            return v[:, :, :, 0:h], v[:, :, :, h:2 * h]

        @block.scalar
        def _(act):
            def hi(ck):
                act.wait_ge(s_raw[ck % RAW], 32 * (ck // RAW + 1))
                if ck >= SPL:
                    act.wait_ge(s_used, ck - SPL + 1)
                act.activation(whi[:, ck % SPL, :], raw[:, ck % RAW, :], ACT.Copy).then_inc(s_hi, 1)

            act.wait_ge(s_vec, 1)
            act.activation(cs[:, :, 0], vec[:, R_C:R_C + KD], ACT.Silu)
            act.activation(cs[:, :, 1], vec[:, R_CCTX:R_CCTX + KD], ACT.Silu).then_inc(s_cs, 1)
            act.preload_act_table_set(EXP_LN)
            act.wait_ge(s_lb, 1)
            act.activation(lbt[:, 1, :], lbt[:, 0, :], ACT.Exp).then_inc(s_lb, 1)
            for k in range(KD):
                act.wait_ge(s_xe, k + 1)
                if k >= 2:
                    act.wait_ge(s_ms, k - 1)
                act.activation(sq[:, k % 2, :], xT[:, k, :], ACT.Square).then_inc(s_sq, 1)
            act.wait_ge(s_ms, KD)
            act.activation(rstd[:, :], bank[3][:, :], ACT.Ln, bias=eps[:, :], scale=1.0 / D).then_inc(s_rs, 1)
            act.wait_ge(s_rs, 1)
            act.activation(rstd[:, :], rstd[:, :], ACT.Exp, scale=-0.5).then_inc(s_rs, 1)
            for k in range(KD):
                act.wait_ge(s_a, 2 * (k + 1))
                act.activation(ahi[:, k, :], xT[:, k, :], ACT.Copy).then_inc(s_ah, 1)
                if k in (4, 9):
                    hi(k // 5)

            UNITS = ((0, 0), (1, 0), (0, 1), (1, 1))

            def gate_exps(pr, i):
                d, h = UNITS[i]
                b = pr % 2
                K = keyq[b][:, h, 2 * d, :]
                act.wait_ge(s_zc, 4 * pr + i + 1)
                if pr >= 2 and i == 0:
                    act.wait_ge(s_em, 2 * pr - 2)
                    act.wait_ge(s_sc, 2 * (2 * pr - 2))
                if 4 * pr + i >= 2:
                    act.wait_ge(s_zy, 2 * (4 * pr + i - 1))
                act.activation(K, gates[b][:, h, d, :], ACT.Exp, scale=-1.0).then_inc(s_ze, 1)
                act.wait_ge(s_ze, 3 * (4 * pr + i) + 1)
                act.activation(zt[:, i % 2, 0, :], K, ACT.Ln, bias=1.0).then_inc(s_ze, 1)
                act.activation(zt[:, i % 2, 1, :], K, ACT.Ln, bias=1.0,
                               scale=lbv[:, 2 * pr + h:2 * pr + h + 1]).then_inc(s_ze, 1)

            def gate_sigmoid(pr, i):
                d, h = UNITS[i]
                K = keyq[pr % 2][:, h, 2 * d, :]
                act.wait_ge(s_zy, 2 * (4 * pr + i) + 1)
                act.activation(K, K, ACT.Exp, scale=-1.0).then_inc(s_zk, 1)

            def values_queries(pr):
                b = pr % 2
                act.wait_ge(s_used, 16 * pr + 8)
                if pr >= 2:
                    act.wait_ge(s_o, 2 * pr - 2)
                    act.wait_ge(s_sc, 2 * (2 * pr - 2))
                    act.wait_ge(s_xm, 2 * pr - 2)
                    act.wait_ge(s_em, 2 * pr - 2)
                for i in range(2):
                    act.activation(vals[b][:, 2 * i:2 * i + 2, :],
                                   bank[i][:, :].rearrange("p (t v) -> p t v", t=2), ACT.Copy).then_inc(s_vev, 1)
                act.activation(keyq[b][:, :, 1, T:TT], bank[2][:, :].rearrange("p (h t) -> p h t", h=2),
                               ACT.Silu).then_inc(s_qev, 1)
                act.preload_act_table_set(EXP_LN)

            def scan(j, n):
                m = n % 2
                if j == 1:
                    act.wait_ge(s_cum, n + 1)
                    if n:
                        act.wait_ge(s_tr, 2 * n)
                        act.wait_ge(s_o, n)
                        act.wait_ge(s_s2, n)
                    act.activation(xs[:, 0, 0, :], pcum[:, 0, 0:P], ACT.Exp, bias=tot[:, m, 0, 0:1], scale=-1.0)
                    act.activation(xs[:, 0, 1, :], pcum[:, 0, P:2 * P], ACT.Exp, bias=pcum[:, 0, 2 * P - 1:2 * P], scale=-1.0)
                    act.activation(xs[:, 0, 2, :], pcum[:, 0, 2 * P:3 * P], ACT.Exp, bias=pcum[:, 0, 3 * P - 1:3 * P], scale=-1.0)
                    act.activation(xs[:, 1, 0, :], pcum[:, 1, 0:P], ACT.Exp)
                    act.activation(xs[:, 1, 1, :], pcum[:, 1, P:2 * P], ACT.Exp, bias=tot[:, m, 1, 0:1])
                    act.activation(xs[:, 1, 2, :], pcum[:, 1, 3 * P:TT], ACT.Exp)
                    act.activation(xi[:, 0, :], pcum[:, 0, T:TT], ACT.Exp)
                    for t in range(2):
                        act.activation(xi[:, 1, t * P:(t + 1) * P], pcum[:, 1, T + t * P:T + (t + 1) * P], ACT.Exp,
                                       bias=tot[:, m, 1, 2 + t:3 + t], scale=-1.0)
                    act.activation(etot[:, m, 0:1], pcum[:, 0, 3 * P - 1:3 * P], ACT.Exp)
                    act.activation(etot[:, m, 1:2], tot[:, m, 1, 3:4], ACT.Exp).then_inc(s_ex, 1)
                    act.wait_ge(s_sub, 2 * n + 1)
                    act.activation(eseq[:, :, 0:3 * T], eseq[:, :, 0:3 * T], ACT.Exp).then_inc(s_el, 1)
                if j == 2:
                    act.wait_ge(s_sub, 2 * n + 2)
                    act.activation(eseq[:, :, 3 * T:NL * T], eseq[:, :, 3 * T:NL * T], ACT.Exp).then_inc(s_el, 1)
                if j == 4:
                    for d in range(2):
                        act.wait_ge(s_tr, 2 * n + d + 1)
                        act.activation(kt[:, d, :, :], (mx, ob)[d][:, 0:384].rearrange("p (j t) -> p j t", j=3),
                                       ACT.Copy).then_inc(s_kt, 1)
                if j == 5:
                    act.wait_ge(s_st, n + 1)
                    act.activation(state[:, 0, :, :], mx[:, 0:256].rearrange("p (d v) -> p d v", d=2),
                                   ACT.Copy).then_inc(s_s1, 1)
                if j == 8:
                    act.wait_ge(s_o, n + 1)
                    act.activation(osq, ob[:, 0:T], ACT.Square).then_inc(s_osq, 1)
                if j == 9:
                    act.wait_ge(s_om, n + 1)
                    if n:
                        act.wait_ge(s_on, n)
                    act.activation(rstd[:, 0:T], mx[:, 0:T], ACT.Ln, bias=eps[:, :], scale=1.0 / P).then_inc(s_ol, 1)
                    act.wait_ge(s_ol, n + 1)
                    act.activation(rstd[:, 0:T], rstd[:, 0:T], ACT.Exp, scale=-0.5).then_inc(s_or, 1)

            def gate_silu(u):
                act.wait_ge(s_used, C_G + 8 * (u + 1))
                for i in range(2):
                    if u:
                        act.wait_ge(s_y, 2 * u)
                    else:
                        act.wait_ge(s_zy, 8 * PAIRS)
                    act.activation(zt[:, i, 0, :], bank[2 * (u % 2) + i][:, :], ACT.Silu).then_inc(s_gev, 1)
                act.preload_act_table_set(EXP_LN)

            for ck, kind, u, r, tasks in positions():
                if ck >= 2:
                    hi(ck)
                if 1 <= ck <= PADA:
                    i = ck - 1
                    act.wait_ge(s_aw[i % 2], 16 * (i // 2 + 1))
                    act.activation(aw[:, i % 2, :], aw[:, i % 2, :], ACT.Copy,
                                   scale=cs[:, i % KD, 0:1]).then_inc(s_am, 1)
                if kind == "Z" and r == 0:
                    values_queries(u)
                p = ck % 16
                if p < 3 and 16 <= ck < C_G + 3:
                    pr = ck // 16 - 1
                    if p > 0:
                        for i in (2 * p - 2, 2 * p - 1):
                            gate_sigmoid(pr, i)
                    if p < 2:
                        for i in (2 * p, 2 * p + 1):
                            gate_exps(pr, i)
                if kind == "G" and r == 0 and u:
                    gate_silu(u - 1)
                for j, n in tasks:
                    scan(j, n)
            gate_silu(3)

            for k in range(KD):
                act.wait_ge(s_y, 2 * (k // 4) + (k % 4) // 2 + 1)
                if k >= 2:
                    act.wait_ge(s_used, C_WO + 2 * (k - 1))
                else:
                    act.wait_ge(s_used, C_WO)
                act.activation(yhi[:, k % 2, :], oT[:, k, :], ACT.Copy).then_inc(s_yh, 1)
                hi(C_WO + 2 * k)
                hi(C_WO + 2 * k + 1)
            for k in range(KD):
                act.wait_ge(s_h, k + 1)
                if k >= 2:
                    act.wait_ge(s_hm, k - 1)
                act.activation(sq[:, k % 2, 0:T], hT[:, k, :], ACT.Square).then_inc(s_hq, 1)
            hi(C_FF)
            hi(C_FF + 1)
            act.wait_ge(s_hm, KD)
            act.activation(rstd[:, 0:T], ob[:, 0:T], ACT.Ln, bias=eps[:, :], scale=1.0 / D).then_inc(s_hr, 1)
            act.wait_ge(s_hr, 1)
            act.activation(rstd[:, 0:T], rstd[:, 0:T], ACT.Exp, scale=-0.5).then_inc(s_hr, 1)
            for k in range(KD):
                act.wait_ge(s_ht, 2 * (k + 1))
                act.activation(ahi[:, k, 0:T], zt[:, 0, k % 2, 0:T], ACT.Copy).then_inc(s_ah, 1)
            for u in range(2 * FG):
                for r in range(8):
                    ck = C_FF + 8 * u + r
                    if ck >= C_FF + 2:
                        hi(ck)
                    if r == 0 and u % 2 == 1:
                        j = u // 2
                        act.wait_ge(s_used, C_FF + 8 * u)
                        if j:
                            act.wait_ge(s_fh, 2 * j)
                        for i in range(2):
                            act.activation(sq[:, i, :], bank[i][:, :], ACT.Silu).then_inc(s_fgs, 1)
            act.preload_act_table_set(EXP_LN)
            for k in range(KF):
                act.wait_ge(s_fh, 2 * (k // 4) + (k % 4) // 2 + 1)
                if k >= 2:
                    act.wait_ge(s_used, C_DN + 2 * (k - 1))
                else:
                    act.wait_ge(s_used, C_FF)
                act.activation(yhi[:, k % 2, :], h1[:, k, :], ACT.Copy).then_inc(s_yh, 1)
                hi(C_DN + 2 * k)
                hi(C_DN + 2 * k + 1)
            for k in range(KD):
                act.wait_ge(s_fo, k + 1)
                if k >= 2:
                    act.wait_ge(s_fm, k - 1)
                act.activation(sq[:, k % 2, 0:T], hT[:, k, :], ACT.Square).then_inc(s_fq, 1)
            act.wait_ge(s_fm, KD)
            act.activation(rcol[:, 0, :], bank[1][:, 0:2], ACT.Ln, bias=eps[:, :], scale=1.0 / D).then_inc(s_fr, 1)
            act.wait_ge(s_fr, 1)
            act.activation(rcol[:, 1, :], rcol[:, 0, :], ACT.Exp, scale=-0.5).then_inc(s_fr, 1)

        def hidden(dve, j):
            dve.wait_ge(s_used, C_FF + 16 * (j + 1))
            for i in range(2):
                dve.wait_ge(s_fgs, 2 * j + i + 1)
                k = 4 * j + 2 * i
                dve.tensor_tensor(h1[:, k:k + 2, :], sq[:, i, :].rearrange("p (k t) -> p k t", k=2),
                                  bank[2 + i][:, :].rearrange("p (k t) -> p k t", k=2), ALU.mult).then_inc(s_fh, 1)

        @block.vector
        def _(dve):
            def lo(ck):
                dve.wait_ge(s_hi, ck + 1)
                dve.tensor_tensor(wlo[:, ck % SPL, :], raw[:, ck % RAW, :], whi[:, ck % SPL, :].bitcast(F32),
                                  ALU.subtract).then_inc(s_lo, 1)

            dve.memset(ones[:, :], 1.0)
            dve.memset(eps[:, :], EPS).then_inc(s_one, 1)
            dve.wait_ge(s_vecT, 1)
            dve.tensor_copy(vec[:, :], mx[:, 0:VROWS]).then_inc(s_vec, 1)
            dve.tensor_copy(bias[:, :], mx[:, 128:224]).then_inc(s_vec, 1)
            dve.wait_ge(s_vec, 2)
            lg = vec[:, R_LB:R_LB + KD]
            dve.tensor_tensor(lbt[:, 0, :], lg, lg, ALU.subtract).then_inc(s_lb, 1)
            dve.wait_ge(s_lb, 2)
            dve.reciprocal(lbt[:, 2, :], lbt[:, 1, :]).then_inc(s_lb, 1)
            dve.wait_ge(s_lb, 3)
            dve.tensor_tensor(lbt[:, 0, :], lbt[:, 1, :], lbt[:, 2, :], ALU.mult).then_inc(s_lb, 1)
            dve.wait_ge(s_lb, 4)
            dve.tensor_tensor(lbv, lbt[:, 0, :], lbt[:, 0, :], ALU.subtract).then_inc(s_lb, 1)
            dve.wait_ge(s_lb, 5)
            dve.tensor_scalar(oml[:, :], lbv, -1.0, 1.0, ALU.mult, ALU.add).then_inc(s_mod, 1)
            for k in range(KD):
                dve.wait_ge(s_xt, k + 1)
                dve.tensor_copy(xT[:, k, :], bank[k % 2][:, :]).then_inc(s_xe, 1)
            dve.wait_ge(s_rs, 2)
            dve.wait_ge(s_xs, 16)
            for k in range(KD):
                dve.tensor_tensor(xT[:, k, :], xT[:, k, :], rstd[:, :], ALU.mult).then_inc(s_xn, 1)
            dve.wait_ge(s_ada_used, ADA0)
            am = bank[2][:, 0:64].rearrange("p (m k s) -> p m k s", m=2, s=2)
            b2 = bias[:, 0:2 * KD].rearrange("p (m k) -> p m k", m=2)
            dve.tensor_tensor(mod[:, 0:2, :], am[:, :, :, 0], b2, ALU.add).then_inc(s_mod, 1)
            dve.tensor_tensor(modc[:, :, :], am[:, :, :, 1], b2, ALU.add).then_inc(s_mod, 1)
            dve.wait_ge(s_mod, 3)
            nm = vec[:, R_NMIX:R_NMIX + KD]
            dve.scalar_tensor_tensor(out=scl[:, 0, :], in0=modc[:, 1, :], scalar=1.0, in1=nm, op0=ALU.add,
                                     op1=ALU.mult).then_inc(s_mod, 1)
            dve.scalar_tensor_tensor(out=scl[:, 1, :], in0=mod[:, 1, :], scalar=1.0, in1=nm, op0=ALU.add,
                                     op1=ALU.mult).then_inc(s_mod, 1)
            dve.wait_ge(s_mod, 5)
            dve.wait_ge(s_xn, KD)
            for k in range(KD):
                for i, sh in enumerate((modc[:, 0, k:k + 1], mod[:, 0, k:k + 1])):
                    v = xT[:, k, i * T:(i + 1) * T]
                    dve.tensor_scalar(v, v, scl[:, i, k:k + 1], sh, ALU.mult, ALU.add).then_inc(s_a, 1)
                if k:
                    q = k - 1
                    dve.wait_ge(s_ah, q + 1)
                    dve.tensor_tensor(alo[:, q, :], xT[:, q, :], ahi[:, q, :].bitcast(F32), ALU.subtract).then_inc(s_al, 1)
                if k in (5, 10):
                    lo(k // 5 - 1)
            dve.wait_ge(s_ah, KD)
            dve.tensor_tensor(alo[:, KD - 1, :], xT[:, KD - 1, :], ahi[:, KD - 1, :].bitcast(F32),
                              ALU.subtract).then_inc(s_al, 1)

            UNITS = ((0, 0), (1, 0), (0, 1), (1, 1))

            def clip_gates(pr):
                dve.wait_ge(s_used, 16 * (pr + 1))
                if pr >= 2:
                    dve.wait_ge(s_cum, 2 * pr - 2)
                for i, (d, h) in enumerate(UNITS):
                    dve.tensor_scalar(gates[pr % 2][:, h, d, :], bank[2 * d + h][:, :], -CLIP, CLIP, ALU.max,
                                      ALU.min).then_inc(s_zc, 1)

            def log_gates(pr, i):
                d, h = UNITS[i]
                b = pr % 2
                n = 4 * pr + i
                G, K = gates[b][:, h, d, :], keyq[b][:, h, 2 * d, :]
                dve.wait_ge(s_ze, 3 * n + 3)
                dve.wait_ge(s_zc, n + 1)
                dve.tensor_tensor(K, G, zt[:, i % 2, 0, :], ALU.add).then_inc(s_zy, 1)
                dve.wait_ge(s_zy, 2 * n + 1)
                dve.tensor_tensor(G, zt[:, i % 2, 1, :], zt[:, i % 2, 0, :], ALU.subtract).then_inc(s_zy, 1)

            def keys(pr, i):
                d, h = UNITS[i]
                K = keyq[pr % 2][:, h, 2 * d, :]
                dve.wait_ge(s_zk, 4 * pr + i + 1)
                dve.tensor_scalar(K, K, oml[:, 2 * pr + h:2 * pr + h + 1], None, ALU.mult).then_inc(s_k, 1)

            def scale_queries(pr):
                dve.wait_ge(s_qev, pr + 1)
                Q = keyq[pr % 2][:, :, 1, T:TT]
                dve.tensor_scalar(Q, Q, QSCALE, None, ALU.mult).then_inc(s_qs, 1)

            def levels(n, which):
                for li in which:
                    h = HALVES[li]
                    xl, xr = halves(pcum[:, :, T:TT], h)
                    el, er = halves(ebuf[:, :, li, :], h)
                    nb = T // (2 * h)
                    r = mid_ap(h, nb)
                    dve.tensor_tensor(el, r, xl, ALU.subtract)
                    last = dve.tensor_tensor(er, xr, r, ALU.subtract)
                last.then_inc(s_sub, 1)

            def mid_ap(h, nb):
                full = pcum[:, :, T:TT]
                pstep = full.ap[0]
                return bass.AP(tensor=full.tensor, offset=full.offset + h - 1,
                               ap=[list(pstep), [TT + 1, 2], [2 * h, nb], [0, h]])

            def level_muls(n, which, last_one):
                b, hh = (n // 2) % 2, n % 2
                kq = keyq[b][:, hh, :, T:TT]
                for li in which:
                    h = HALVES[li]
                    el, er = halves(ebuf[:, :, li, :], h)
                    ml, _ = halves(kq[:, 0:2, :], h)
                    _, mr = halves(kq[:, 1:3, :], h)
                    dve.tensor_tensor(el, el, ml, ALU.mult)
                    last = dve.tensor_tensor(er, er, mr, ALU.mult)
                if last_one:
                    last.then_inc(s_em, 1)

            def place(n, d):
                h_of = HALVES
                for li, h in enumerate(h_of):
                    nb = P // (2 * h)
                    dst = pT.rearrange("p t (b n) -> p t b n", n=2 * h)
                    dst = dst[:, :, :, h:2 * h] if d == 0 else dst[:, :, :, 0:h]
                    src = score[:, :, li * 64:(li + 1) * 64].rearrange("p t (b n) -> p t b n", n=h)
                    m = masks[:, (d * NL + li) * 64:(d * NL + li + 1) * 64].rearrange("p (b n) -> p b n", n=h)
                    mm = bass.AP(tensor=m.tensor, offset=m.offset, ap=[list(m.ap[0]), [0, 2], [h, nb], [1, h]])
                    dve.copy_predicated(dst, mm, src).then_inc(s_pl, 1)
                    dve.wait_ge(s_pl, (2 * n + d) * NL + li + 1)

            def scan(j, n):
                b, hh, m = (n // 2) % 2, n % 2, n % 2
                G, KQ = gates[b], keyq[b]
                if j == 0:
                    dve.wait_ge(s_k, 4 * (n // 2) + 2 * hh + 2)
                    dve.wait_ge(s_zy, 2 * (4 * (n // 2) + 2 * hh + 2))
                    dve.wait_ge(s_qs, n // 2 + 1)
                    if n:
                        dve.wait_ge(s_ex, n)
                        dve.wait_ge(s_sub, 2 * n)
                    if n >= 2:
                        dve.wait_ge(s_s2, n - 1)
                    dve.tensor_tensor_scan(pcum[:, 0, :], keep[:, :], G[:, hh, 0, :], 0.0, ALU.mult, ALU.add)
                    g1 = G[:, hh, 1, :]
                    shifted = bass.AP(tensor=g1.tensor, offset=g1.offset - 1, ap=[list(a) for a in g1.ap])
                    dve.tensor_tensor_scan(pcum[:, 1, :], shifted, keep[:, :], 0.0, ALU.add, ALU.mult).then_inc(s_cd, 1)
                    dve.wait_ge(s_cd, n + 1)
                    dve.tensor_tensor(tot[:, m, 0, 0:1], pcum[:, 0, P - 1:P], pcum[:, 0, 2 * P - 1:2 * P], ALU.add)
                    ends = slice(P - 1, TT, P)
                    dve.tensor_tensor(tot[:, m, 1, 0:4], pcum[:, 1, ends], G[:, hh, 1, ends], ALU.add).then_inc(s_cum, 1)
                    if n:
                        dve.wait_ge(s_sc, 2 * n)
                    dve.tensor_tensor(ksum, KQ[:, hh, 0, T:TT], KQ[:, hh, 2, T:TT], ALU.add)
                    levels(n, (0, 1, 2))
                if j == 1:
                    levels(n, (3, 4, 5, 6))
                if j == 2:
                    dve.wait_ge(s_ex, n + 1)
                    dve.tensor_tensor(xs[:, 0, :, :], xs[:, 0, :, :],
                                      KQ[:, hh, 0, 0:3 * P].rearrange("p (j t) -> p j t", j=3), ALU.mult)
                    dve.tensor_tensor(xs[:, 1, 0:2, :], xs[:, 1, 0:2, :],
                                      KQ[:, hh, 2, 0:2 * P].rearrange("p (j t) -> p j t", j=2), ALU.mult)
                    dve.tensor_tensor(xs[:, 1, 2, :], xs[:, 1, 2, :], KQ[:, hh, 2, 3 * P:TT], ALU.mult)
                    for d in range(2):
                        last = dve.tensor_tensor(xi[:, d, :], xi[:, d, :], KQ[:, hh, 1, T:TT], ALU.mult)
                    last.then_inc(s_xm, 1)
                    dve.wait_ge(s_el, 2 * n + 1)
                    level_muls(n, (0, 1), False)
                if j == 3:
                    dve.wait_ge(s_el, 2 * n + 2)
                    level_muls(n, (2, 3, 4, 5, 6), True)
                if j == 5:
                    dve.wait_ge(s_s1, n + 1)
                    for d in range(2):
                        last = dve.scalar_tensor_tensor(out=state[:, 1, d, :], in0=state[:, 0, d, :],
                                                        scalar=etot[:, m, d:d + 1],
                                                        in1=mx[:, 256 + d * P:384 + d * P], op0=ALU.mult, op1=ALU.add)
                    last.then_inc(s_s2, 1)
                if j == 6:
                    dve.wait_ge(s_sc, 2 * n + 1)
                    if n:
                        dve.wait_ge(s_o, n)
                    idb = ident[:, :]
                    idb = bass.AP(tensor=idb.tensor, offset=idb.offset, ap=[list(idb.ap[0]), [0, 2], [1, P]])
                    dve.tensor_tensor(pT, ob[:, 0:T].rearrange("p (t n) -> p t n", t=2), idb, ALU.mult).then_inc(s_dg, 1)
                    dve.wait_ge(s_dg, n + 1)
                    place(n, 0)
                if j == 7:
                    dve.wait_ge(s_sc, 2 * n + 2)
                    place(n, 1)
                if j == 10:
                    dve.wait_ge(s_or, n + 1)
                    dve.scalar_tensor_tensor(out=oT[:, n, :], in0=ob[:, 0:T], scalar=vec[:, R_ONORM:R_ONORM + 1],
                                             in1=rstd[:, 0:T], op0=ALU.mult, op1=ALU.mult).then_inc(s_on, 1)

            def gate_outputs(u):
                for i in range(2):
                    dve.wait_ge(s_gev, 2 * u + i + 1)
                    dve.wait_ge(s_on, 4 * u + 2 * i + 2)
                    v = oT[:, 4 * u + 2 * i:4 * u + 2 * i + 2, :]
                    dve.tensor_tensor(v, v, zt[:, i, 0, :].rearrange("p (k t) -> p k t", k=2), ALU.mult).then_inc(s_y, 1)

            def add_modulation(e):
                dve.wait_ge(s_ap, e + 1)
                v = mod[:, 2 + e // 2, (e % 2) * 8:(e % 2) * 8 + 8]
                o = 2 * KD + 8 * e
                dve.tensor_tensor(v, bank[3][:, 0:8], bias[:, o:o + 8], ALU.add).then_inc(s_av, 1)

            for ck, kind, u, r, tasks in positions():
                if ck >= 2:
                    lo(ck)
                if kind == "Z" and r == 1:
                    scale_queries(u)
                p = ck % 16
                if p < 4 and 16 <= ck < C_G + 4:
                    pr = ck // 16 - 1
                    if p == 0:
                        clip_gates(pr)
                    if p in (1, 2):
                        for i in (2 * p - 2, 2 * p - 1):
                            log_gates(pr, i)
                    if p in (2, 3):
                        for i in (2 * p - 4, 2 * p - 3):
                            keys(pr, i)
                if kind == "G" and r == 1 and u:
                    gate_outputs(u - 1)
                if ADA_AT(ck) is not None:
                    add_modulation(ADA_AT(ck))
                for j, n in tasks:
                    scan(j, n)
            gate_outputs(3)

            for k in range(KD):
                dve.wait_ge(s_yh, k + 1)
                dve.wait_ge(s_y, 2 * (k // 4) + (k % 4) // 2 + 1)
                dve.tensor_tensor(ylo[:, k % 2, :], oT[:, k, :], yhi[:, k % 2, :].bitcast(F32), ALU.subtract).then_inc(s_yl, 1)
                lo(C_WO + 2 * k)
                lo(C_WO + 2 * k + 1)
            dve.wait_ge(s_av, 8)
            dve.scalar_tensor_tensor(out=sclf[:, :], in0=mod[:, 4, :], scalar=1.0, in1=vec[:, R_NFFN:R_NFFN + KD],
                                     op0=ALU.add, op1=ALU.mult).then_inc(s_mod, 1)
            dve.wait_ge(s_used, C_FF)
            dve.wait_ge(s_xb, 16)
            for k in range(KD):
                dve.scalar_tensor_tensor(out=hT[:, k, :], in0=all8[k // 2][:, (k % 2) * T:(k % 2) * T + T],
                                         scalar=mod[:, 2, k:k + 1], in1=xres[:, k, :], op0=ALU.mult,
                                         op1=ALU.add).then_inc(s_h, 1)
            lo(C_FF)
            lo(C_FF + 1)
            dve.wait_ge(s_hr, 2)
            dve.wait_ge(s_mod, 6)
            for k in range(KD):
                if k >= 2:
                    dve.wait_ge(s_al, KD + k - 1)
                t, a = zt[:, 1, k % 2, 0:T], zt[:, 0, k % 2, 0:T]
                dve.wait_ge(s_h, k + 1)
                dve.tensor_tensor(t, hT[:, k, :], rstd[:, 0:T], ALU.mult).then_inc(s_ht, 1)
                dve.wait_ge(s_ht, 2 * k + 1)
                dve.tensor_scalar(a, t, sclf[:, k:k + 1], mod[:, 3, k:k + 1], ALU.mult, ALU.add).then_inc(s_ht, 1)
                dve.wait_ge(s_ah, KD + k + 1)
                dve.wait_ge(s_ht, 2 * k + 2)
                dve.tensor_tensor(alo[:, k, 0:T], a, ahi[:, k, 0:T].bitcast(F32), ALU.subtract).then_inc(s_al, 1)
            for u in range(2 * FG):
                for r in range(8):
                    ck = C_FF + 8 * u + r
                    if ck >= C_FF + 2:
                        lo(ck)
                    if r == 0 and u % 2 == 0 and u:
                        hidden(dve, u // 2 - 1)
            hidden(dve, FG - 1)
            for k in range(KF):
                dve.wait_ge(s_yh, KD + k + 1)
                dve.wait_ge(s_fh, 2 * (k // 4) + (k % 4) // 2 + 1)
                dve.tensor_tensor(ylo[:, k % 2, :], h1[:, k, :], yhi[:, k % 2, :].bitcast(F32), ALU.subtract).then_inc(s_yl, 1)
                lo(C_DN + 2 * k)
                lo(C_DN + 2 * k + 1)
            dve.wait_ge(s_used, CHUNKS)
            for k in range(KD):
                dve.scalar_tensor_tensor(out=hT[:, k, :], in0=all8[k // 2][:, (k % 2) * T:(k % 2) * T + T],
                                         scalar=mod[:, 5, k:k + 1], in1=hT[:, k, :], op0=ALU.mult,
                                         op1=ALU.add).then_inc(s_fo, 1)
            for k in range(KD):
                dve.wait_ge(s_fq, k + 1)
                dve.wait_ge(s_fo, k + 1)
                dve.tensor_scalar(hT[:, k, :], hT[:, k, :], vec[:, R_FIN + k:R_FIN + k + 1], None,
                                  ALU.mult).then_inc(s_fs, 1)
            dve.wait_ge(s_fr, 2)
            for t in range(2):
                for q in range(4):
                    i = 4 * t + q
                    dve.wait_ge(s_ft, i + 1)
                    dve.tensor_scalar(outb[:, t, q * 512:(q + 1) * 512], all8[2 + i % 6], rcol[:, 1, t:t + 1], None,
                                      ALU.mult).then_inc(s_fe, 1)

        def mean_square(pe, k):
            pe.wait_ge(s_one, 1)
            pe.wait_ge(s_sq, k + 1)
            pe.matmul(bank[3][:, :], ones[:, :], sq[:, k % 2, :], start=(k == 0), stop=(k == KD - 1)).then_inc(s_ms, 1)


        @block.tensor
        def _(pe):
            pe.wait_ge(s_const, 16 * 11)
            pe.transpose(mx[:, 0:VROWS], vrow[0:VROWS, :], ident[0:VROWS, 0:VROWS])
            pe.transpose(mx[:, 128:224], brow[0:96, :], ident[0:96, 0:96]).then_inc(s_vecT, 1)
            for t in range(4):
                pe.wait_ge(s_x[t], 16)
            for k in range(KD):
                if k >= 2:
                    pe.wait_ge(s_xe, k - 1)
                for t in range(4):
                    last = pe.transpose(bank[k % 2][:, t * P:(t + 1) * P], xin[:, t, k * P:(k + 1) * P], ident[:, :])
                last.then_inc(s_xt, 1)
                if k >= 1:
                    mean_square(pe, k - 1)
            mean_square(pe, KD - 1)
            pe.wait_ge(s_cs, 1)
            for i in range(ADA0):
                k, q = divmod(i, 4)
                pe.wait_ge(s_ada_in[i % RAW], 16 * (i // RAW + 1))
                for f in range(8):
                    o = 2 * (8 * q + f)
                    last = pe.matmul(bank[2][:, o:o + 2], raw[:, i % RAW, f * P:(f + 1) * P], cs[:, k, :],
                                     start=(i == 0 and f == 0), stop=(k == KD - 1), skip_group_check=True)
                last.then_inc(s_ada_used, 1)

            def three(dst, w, wl, ah, al, start, stop):
                pe.matmul(dst, w, ah, start=start, stop=False, skip_group_check=True)
                pe.matmul(dst, w, al, start=False, stop=False, skip_group_check=True)
                return pe.matmul(dst, wl, ah, start=False, stop=stop, skip_group_check=True)

            def chunk(ck, kind, r, u=0):
                s = ck % SPL
                for a in range(2):
                    k = 2 * r + a
                    first, end = k == 0, k == KD - 1
                    if ck < 8 and kind == "VQ":
                        pe.wait_ge(s_al, k + 1)
                    if kind == "FF" and u == 0:
                        pe.wait_ge(s_al, KD + k + 1)
                    if kind == "VQ":
                        for t in range(4):
                            dst = bank[t // 2][:, (t % 2) * T:(t % 2 + 1) * T]
                            o = slice(512 * a, 512 * a + 256)
                            tk = slice(t * P, (t + 1) * P)
                            st = first and t % 2 == 0
                            pe.matmul(dst, ahi[:, k, tk], whi[:, s, o], start=st, stop=False, skip_group_check=True)
                            pe.matmul(dst, ahi[:, k, tk], wlo[:, s, o], start=False, stop=False, skip_group_check=True)
                            pe.matmul(dst, alo[:, k, tk], whi[:, s, o], start=False, stop=end, skip_group_check=True)
                        for f in range(2):
                            o = slice(512 * a + 256 + f * P, 512 * a + 256 + (f + 1) * P)
                            last = three(bank[2][:, f * T:(f + 1) * T], whi[:, s, o], wlo[:, s, o], ahi[:, k, T:TT],
                                         alo[:, k, T:TT], first and f == 0, end)
                    elif kind == "Z":
                        for f in range(4):
                            if first:
                                if f == 0:
                                    pass
                            o = slice(512 * a + f * P, 512 * a + (f + 1) * P)
                            last = three(bank[f][:, :], whi[:, s, o], wlo[:, s, o], ahi[:, k, :], alo[:, k, :], first, end)
                    else:
                        tk = slice(T, TT) if kind == "G" else slice(0, T)
                        bb = 2 * (u % 2)
                        for f in range(4):
                            o = slice(512 * a + f * P, 512 * a + (f + 1) * P)
                            last = three(bank[bb + f // 2][:, (f % 2) * T:(f % 2 + 1) * T], whi[:, s, o], wlo[:, s, o],
                                         ahi[:, k, tk], alo[:, k, tk], first and f % 2 == 0, end)
                last.then_inc(s_used, 1)

            def wide(ck, i, half, k_end):
                s = ck % SPL
                for f in range(8):
                    ft = 8 * half + f
                    o = slice(f * P, (f + 1) * P)
                    last = three(all8[ft // 2][:, (ft % 2) * T:(ft % 2 + 1) * T], whi[:, s, o], wlo[:, s, o],
                                 yhi[:, i % 2, :], ylo[:, i % 2, :], i == 0 and ft % 2 == 0, i == k_end)
                last.then_inc(s_used, 1)

            def scan(j, n):
                b, hh = (n // 2) % 2, n % 2
                KQ = keyq[b]
                V = vals[b][:, :, hh * P:(hh + 1) * P]
                if j == 3:
                    pe.wait_ge(s_xm, n + 1)
                    for d in range(2):
                        if n:
                            pe.wait_ge(s_on, n)
                            pe.wait_ge(s_or, n)
                        for i in range(3):
                            last = pe.transpose((mx, ob)[d][:, i * P:(i + 1) * P], xs[:, d, i, :], ident[:, :])
                        last.then_inc(s_tr, 1)
                if j == 4:
                    pe.wait_ge(s_kt, 2 * n + 2)
                    pe.wait_ge(s_vev, 2 * (n // 2) + 2)
                    for d in range(2):
                        for t in range(2):
                            pe.matmul(mx[:, d * P:(d + 1) * P], kt[:, d, t, :], V[:, t, :], start=(t == 0), stop=(t == 1))
                    for d in range(2):
                        last = pe.matmul(mx[:, 256 + d * P:384 + d * P], kt[:, d, 2, :], V[:, 2 + d, :], start=True, stop=True)
                    last.then_inc(s_st, 1)
                if j in (5, 6):
                    d = j - 5
                    pe.wait_ge(s_em, n + 1)
                    if d == 1:
                        pe.wait_ge(s_pl, (2 * n + 1) * NL)
                    elif n:
                        pe.wait_ge(s_pl, 2 * n * NL)
                    for t in range(2):
                        for li, h in enumerate(HALVES):
                            e = ebuf[:, d, li, t * P:(t + 1) * P]
                            q = e.rearrange("p (b n) -> p b n", n=2 * h)
                            q = q[:, :, h:2 * h] if d == 0 else q[:, :, 0:h]
                            last = pe.matmul(score[:, t, li * 64:(li + 1) * 64], e, q, start=True, stop=True)
                    if d == 0:
                        for t in range(2):
                            last = pe.matmul(ob[:, t * P:(t + 1) * P], ksum[:, t * P:(t + 1) * P],
                                             KQ[:, hh, 1, T + t * P:T + (t + 1) * P], start=True, stop=True)
                    last.then_inc(s_sc, 1)
                if j == 7:
                    pe.wait_ge(s_pl, (2 * n + 2) * NL)
                    pe.wait_ge(s_s2, n + 1)
                    for t in range(2):
                        o = ob[:, t * P:(t + 1) * P]
                        pe.matmul(o, V[:, 2 + t, :], pT[:, t, :], start=True, stop=False)
                        pe.matmul(o, state[:, t, 0, :], xi[:, 0, t * P:(t + 1) * P], start=False, stop=False)
                        last = pe.matmul(o, state[:, 1 - t, 1, :], xi[:, 1, t * P:(t + 1) * P], start=False, stop=True)
                    last.then_inc(s_o, 1)
                if j == 8:
                    pe.wait_ge(s_osq, n + 1)
                    pe.matmul(mx[:, 0:T], ones[:, :], osq, start=True, stop=True).then_inc(s_om, 1)

            def sum_modulation(e):
                pe.wait_ge(s_ac, KD * (e + 1))
                for f in range(8):
                    last = pe.matmul(bank[3][:, f:f + 1], aacc[:, f * P:(f + 1) * P], ones[:, 0:1], start=True, stop=True)
                last.then_inc(s_ap, 1)

            for ck, kind, u, r, tasks in positions():
                if kind == "VQ" and r == 0 and u:
                    pe.wait_ge(s_zc, 4 * u)
                if kind == "Z" and r == 0:
                    pe.wait_ge(s_vev, 2 * (u + 1))
                    pe.wait_ge(s_qev, u + 1)
                    if u:
                        pe.wait_ge(s_av, u)
                if kind == "G" and r == 0:
                    if u == 0:
                        pe.wait_ge(s_zc, 4 * PAIRS)
                    elif u >= 2:
                        pe.wait_ge(s_gev, 2 * (u - 1))
                    if u == 1:
                        pe.wait_ge(s_av, 8)
                pe.wait_ge(s_lo, ck + 1)
                chunk(ck, kind, r, u)
                for j, n in tasks:
                    scan(j, n)
                if SUM_AT(ck) is not None:
                    sum_modulation(SUM_AT(ck))
            pe.wait_ge(s_on, HEADS)
            pe.wait_ge(s_gev, 8)
            for k in range(KD):
                pe.wait_ge(s_yl, k + 1)
                for half in range(2):
                    ck = C_WO + 2 * k + half
                    pe.wait_ge(s_lo, ck + 1)
                    wide(ck, k, half, KD - 1)
            for k in range(KD):
                pe.wait_ge(s_hq, k + 1)
                if k == 0:
                    pe.wait_ge(s_h, KD)
                pe.matmul(ob[:, 0:T], ones[:, :], sq[:, k % 2, 0:T], start=(k == 0), stop=(k == KD - 1)).then_inc(s_hm, 1)
            for u in range(2 * FG):
                j = u // 2
                if j:
                    if u % 2 == 0:
                        pe.wait_ge(s_fgs, 2 * j)
                    else:
                        pe.wait_ge(s_fh, 2 * j)
                for r in range(8):
                    ck = C_FF + 8 * u + r
                    pe.wait_ge(s_lo, ck + 1)
                    chunk(ck, "FF", r, u)
            pe.wait_ge(s_fh, 2 * FG)
            pe.wait_ge(s_hr, 1)
            for k in range(KF):
                pe.wait_ge(s_yl, KD + k + 1)
                for half in range(2):
                    ck = C_DN + 2 * k + half
                    pe.wait_ge(s_lo, ck + 1)
                    wide(ck, k, half, KF - 1)
            for k in range(KD):
                pe.wait_ge(s_fq, k + 1)
                if k == 0:
                    pe.wait_ge(s_fo, KD)
                for t in range(2):
                    last = pe.matmul(bank[1][:, t:t + 1], sq[:, k % 2, t * P:(t + 1) * P], ones[:, 0:1],
                                     start=(k == 0 and t == 0), stop=(k == KD - 1), skip_group_check=True)
                last.then_inc(s_fm, 1)
            for t in range(2):
                for q in range(4):
                    i = 4 * t + q
                    if i >= 6:
                        pe.wait_ge(s_fe, i - 5)
                    for f in range(4):
                        k = 4 * q + f
                        pe.wait_ge(s_fs, k + 1)
                        last = pe.transpose(all8[2 + i % 6][:, f * P:(f + 1) * P], hT[:, k, t * P:(t + 1) * P], ident[:, :])
                    last.then_inc(s_ft, 1)

def SUM_AT(ck):
    e, p = divmod(ck, 16)
    return e - 1 if p == 1 and 1 <= e <= 8 and ck < C_G + 16 else None


def ADA_AT(ck):
    e, p = divmod(ck, 16)
    return e - 1 if p == 2 and 1 <= e <= 8 and ck < C_G + 16 else None


def shape_constants():
    ident = np.eye(P, dtype=np.float32)
    keep = np.ones((P, TT), np.float32)
    keep[:, ::P] = 0.0
    masks = np.zeros((P, 2, NL, 64), np.uint32)
    s = np.arange(P)[:, None]
    j = np.arange(64)[None, :]
    for li, h in enumerate(HALVES):
        for d in range(2):
            t = (j // h) * 2 * h + j % h + (h if d == 0 else 0)
            same = s // (2 * h) == t // (2 * h)
            left = s % (2 * h) < h
            masks[:, d, li, :] = same & (left if d == 0 else ~left)
    return ident, keep, masks.reshape(P, 2 * NL * 64)


_INS = ["x", "c", "ctx", "c_ctx", "w_ada", "b_ada", "norm_mix", "norm_ffn", "hg_lb_logits", "hg_w_in", "hg_w_f",
        "hg_o_norm", "hg_w_o", "ffn_w_gate", "ffn_w_up", "ffn_w_down", "final_norm"]


def kernel(**inputs):
    import numpy as _np
    import concourse.bacc as _bacc
    from concourse import mybir as _mybir
    from concourse.bass_utils import run_bass_kernel_spmd as _run

    nc = _bacc.Bacc("TRN2", target_bir_lowering=False, num_devices=1, dynamic_dma_scratch_size=1024)
    arrays, args = {}, []
    ident, keep, masks = shape_constants()
    named = [(n, _np.ascontiguousarray(inputs[n])) for n in _INS]
    named += [("ident", ident), ("keep", keep), ("masks", masks)]
    for name, a in named:
        arrays[f"in_{name}_dram"] = a
        args.append(nc.dram_tensor(f"in_{name}_dram", a.shape, _mybir.dt.from_np(a.dtype), kind="ExternalInput").ap())
    args.append(nc.dram_tensor("out_0_dram", (1, T, D), _mybir.dt.float32, kind="ExternalOutput").ap())
    build(nc, *args)
    r = _run(nc, [arrays], core_ids=[0])
    return r.results[0]["out_0_dram"]
```

```python
from contextlib import ExitStack

import numpy as np

import concourse.bass as bass
from concourse import mybir

F32 = mybir.dt.float32
F32R = mybir.dt.float32r
U32 = mybir.dt.uint32
ALU = mybir.AluOpType
ACT = mybir.ActivationFunctionType
EXP_LN = "natural_log_exp_and_others"

P = 128
D = 2048
T = 256
TT = 2 * T
KD = D // P
HEADS = 16
PAIRS = HEADS // 2
GROUPS = PAIRS // 2
HALVES = [64, 32, 16, 8, 4, 2, 1]
NL = len(HALVES)
FF = 5632
KF = FF // P
FG = FF // 512
EPS = 1e-6
CLIP = 30.0
QSCALE = float(P) ** -0.5

CW = 1024
RAW = 4
SPL = 2
BODY = 32
C_B = KD * 4
C_G = C_B + GROUPS * BODY
C_WO = C_G + 4 * 8
C_FF = C_WO + KD * 2
C_DN = C_FF + FG * 16
CHUNKS = C_DN + KF * 2
PADA = 8 * KD

R_NMIX, R_NFFN, R_FIN, R_LB, R_C, R_CCTX, R_ONORM = 0, 16, 32, 48, 64, 80, 96
VROWS = 97


def head_slots():
    return [(-5, -3), (3, -2), (11, -1), (19, 0), (27, 1)]


def tasks_at(p, groups=True):
    return [(p - s, off) for s, off in head_slots() if 0 <= p - s <= 11]


def tasks_tail(p):
    out = []
    for s, head, stretched in ((-5, HEADS - 3, False), (3, HEADS - 2, True), (15, HEADS - 1, True)):
        for j in range(12):
            at = s + (3 * j) // 2 if stretched else s + j
            if at == p:
                out.append((j, head))
    return out


def positions():
    for g in range(GROUPS):
        for p in range(BODY):
            kind = "Z" if p % 16 >= 8 else "VQ"
            tasks = [(j, 4 * g + off) for j, off in tasks_at(p) if 4 * g + off >= 0]
            yield C_B + g * BODY + p, kind, 2 * g + p // 16, p % 8, tasks
    for p in range(32):
        yield C_G + p, "G", p // 8, p % 8, tasks_tail(p)


def build(nc, x, c, ctx, c_ctx, w_ada, b_ada, norm_mix, norm_ffn, lb_logits, w_in, w_f, o_norm, w_o,
          w_gate, w_up, w_down, final_norm, ident_in, keep_in, masks_in, out):
    xrows = x.rearrange("b (t p) d -> (b t) p d", p=P)
    crows = ctx.rearrange("b (t p) d -> (b t) p d", p=P)
    orows = out.rearrange("b (t p) d -> (b t) p d", p=P)
    wada = w_ada[0].rearrange("(k p) n -> k p n", p=P)
    win = w_in[0].rearrange("(k p) n -> p k n", p=P)
    wf = [w_f[0, d].rearrange("(k p) n -> p k n", p=P) for d in range(2)]
    wo = w_o[0].rearrange("(k p) n -> k p n", p=P)
    wgu = [w[0].rearrange("(k p) n -> p k n", p=P) for w in (w_gate, w_up)]
    wdn = w_down[0].rearrange("(k p) n -> k p n", p=P)

    stack = ExitStack()
    with stack:
        def sb(name, shape, dt=F32):
            return stack.enter_context(nc.sbuf_tensor(name, shape, dt))

        def sem(name):
            return stack.enter_context(nc.semaphore(name))

        raw = sb("raw", [P, RAW, CW])
        whi = sb("whi", [P, SPL, CW], F32R)
        wlo = sb("wlo", [P, SPL, CW], F32R)
        ahi = sb("ahi", [P, KD, TT], F32R)
        alo = sb("alo", [P, KD, TT], F32R)
        arena = sb("arena", [P, 2 * 6144])
        xin = arena[:, 0:4 * D].rearrange("p (t d) -> p t d", t=4)
        h1 = arena[:, 0:KF * T].rearrange("p (k t) -> p k t", k=KF)
        outb = arena[:, 0:2 * D].rearrange("p (t d) -> p t d", t=2)
        pair = [arena[:, b * 6144:(b + 1) * 6144] for b in range(2)]
        gates = [a[:, 0:2048].rearrange("p (h d t) -> p h d t", h=2, d=2) for a in pair]
        keyq = [a[:, 2048:5120].rearrange("p (h s t) -> p h s t", h=2, s=3) for a in pair]
        vals = [a[:, 5120:6144].rearrange("p (t v) -> p t v", t=4) for a in pair]
        work = sb("work", [P, 4096 + 7680])
        oT = work[:, 0:4096].rearrange("p (k t) -> p k t", k=KD)
        hT = oT
        xT = work[:, 0:KD * TT].rearrange("p (k t) -> p k t", k=KD)
        ebuf = work[:, 4096:4096 + 3584].rearrange("p (d l t) -> p d l t", d=2, l=NL)
        eseq = work[:, 4096:4096 + 3584].rearrange("p (d n) -> p d n", d=2)
        pcum = work[:, 7680:8704].rearrange("p (d t) -> p d t", d=2)
        xs = work[:, 8704:9472].rearrange("p (d j t) -> p d j t", d=2, j=3)
        xi = work[:, 9472:9984].rearrange("p (d t) -> p d t", d=2)
        kt = work[:, 9984:10752].rearrange("p (d j t) -> p d j t", d=2, j=3)
        state = work[:, 10752:11264].rearrange("p (o d v) -> p o d v", o=2, d=2)
        pT = work[:, 11264:11520].rearrange("p (t n) -> p t n", t=2)
        ksum = work[:, 11520:11776]
        xres = work[:, 4096:8192].rearrange("p (k t) -> p k t", k=KD)

        rstd = sb("rstd", [P, TT])
        zt = sb("zt", [P, 2, 2, TT])
        sq = zt[:, :, 0, :]
        osq = rstd[:, T:TT]
        aw = sb("aw", [P, 2, CW])
        aacc = sb("aacc", [P, CW])
        yhi = ahi[:, 0:2, T:TT]
        ylo = alo[:, 0:2, T:TT]
        ident = sb("ident", [P, P])
        ones = sb("ones", [P, P])
        keep = sb("keep", [P, TT])
        masks = sb("masks", [P, 2 * NL * 64], U32)
        vrow = arena[:, 4 * D:4 * D + P]
        brow = arena[:, 4 * D + P:4 * D + 2 * P]
        vec = sb("vec", [P, VROWS])
        bias = sb("bias", [P, 96])
        eps = sb("eps", [P, 1])
        cs = sb("cs", [P, KD, 2])
        cs4 = sb("cs4", [P, KD, 2, 2], F32R)
        mod = sb("mod", [P, 6, KD])
        modc = sb("modc", [P, 2, KD])
        arow = aacc[0:4, :]
        scl = sb("scl", [P, 2, KD])
        sclf = sb("sclf", [P, KD])
        lbt = sb("lbt", [P, 4, KD])
        lbv = lbt[:, 3, :]
        oml = sb("oml", [P, KD])
        tot = sb("tot", [P, 2, 2, 8])
        etot = sb("etot", [P, 2, 2])
        rcol = sb("rcol", [P, 2, 2])
        xdram = nc.dram_tensor("x_features", [P, KD * T], F32, kind="Internal").ap()

        bank = [stack.enter_context(nc.psum_tensor(f"bank{i}", [P, 512], F32)) for i in range(4)]
        score = stack.enter_context(nc.psum_tensor("score", [P, 2, 512], F32))
        mx = stack.enter_context(nc.psum_tensor("mx", [P, 512], F32))
        ob = stack.enter_context(nc.psum_tensor("ob", [P, 512], F32))
        all8 = [b[:, :] for b in bank] + [score[:, 0, :], score[:, 1, :], mx[:, :], ob[:, :]]

        s_const = sem("const_in")
        s_x = [sem(f"x_in{t}") for t in range(4)]
        s_vecT = sem("vectors_turned")
        s_vec = sem("vectors_ready")
        s_one = sem("ones_ready")
        s_cs = sem("silu_c_ready")
        s_lb = sem("lower_bound_steps")
        s_c4 = sem("silu_c_split")
        s_ar = sem("mod_rows_ready")
        s_at = sem("mod_rows_turned")
        s_xt = sem("x_turned")
        s_xe = sem("x_evacuated")
        s_sq = sem("x_squared")
        s_ms = sem("x_mean_square")
        s_rs = sem("x_rstd")
        s_xs = sem("x_stored")
        s_xn = sem("x_normed")
        s_mod = sem("mod_steps")
        s_a = sem("a_value")
        s_ah = sem("a_hi")
        s_al = sem("a_lo")
        s_raw = [sem(f"raw_in{i}") for i in range(RAW)]
        s_hi = sem("hi_ready")
        s_lo = sem("lo_ready")
        s_used = sem("chunk_used")
        s_aw = [sem(f"aw_in{i}") for i in range(2)]
        s_az = sem("ada_cleared")
        s_am = sem("ada_products")
        s_ac = sem("ada_accumulated")
        s_ap = sem("ada_summed")
        s_av = sem("ada_evacuated")
        s_vev = sem("v_evacuated")
        s_qev = sem("q_evacuated")
        s_qs = sem("q_scaled")
        s_zc = sem("z_clipped")
        s_ze = sem("z_exps")
        s_zy = sem("z_log_f")
        s_zk = sem("z_sigmoid")
        s_k = sem("keys_ready")
        s_cd = sem("cumulated")
        s_cum = sem("totals_ready")
        s_sub = sem("exponents")
        s_ex = sem("state_exps")
        s_el = sem("level_exps")
        s_xm = sem("state_operands")
        s_em = sem("level_operands")
        s_tr = sem("keys_turned")
        s_kt = sem("turned_keys_ready")
        s_st = sem("states_summed")
        s_s1 = sem("first_state_ready")
        s_s2 = sem("second_state_ready")
        s_sc = sem("scores_ready")
        s_dg = sem("diagonal_placed")
        s_pl = sem("scores_placed")
        s_o = sem("outputs_ready")
        s_osq = sem("outputs_squared")
        s_om = sem("outputs_mean_square")
        s_ol = sem("outputs_ln")
        s_or = sem("outputs_rstd")
        s_on = sem("outputs_normed")
        s_gev = sem("gate_evacuated")
        s_y = sem("y_gated")
        s_yh = sem("y_hi")
        s_yl = sem("y_lo")
        s_wo = sem("wo_summed")
        s_xb = sem("x_back")
        s_h = sem("h_ready")
        s_hq = sem("h_squared")
        s_hm = sem("h_mean_square")
        s_hr = sem("h_rstd")
        s_ht = sem("h_scaled")
        s_fa = sem("ffn_in")
        s_fg = sem("ffn_gate")
        s_fgs = sem("ffn_gate_silu")
        s_fh = sem("ffn_hidden")
        s_dn = sem("down_summed")
        s_fo = sem("final_h")
        s_fq = sem("final_squared")
        s_fm = sem("final_mean_square")
        s_fr = sem("final_rstd")
        s_fs = sem("final_scaled")
        s_ft = sem("final_turned")
        s_fe = sem("final_evacuated")
        s_out = sem("out_stored")

        block = stack.enter_context(nc.Block())

        def unit_of(ck):
            return (ck - C_FF) // 8

        @block.sync
        def _(sp):
            for dst, src in ((ident, ident_in), (keep, keep_in), (masks, masks_in)):
                sp.dma_start(dst[:, :], src).then_inc(s_const, 16)
            rows = ((R_NMIX, norm_mix[0]), (R_NFFN, norm_ffn[0]), (R_FIN, final_norm), (R_LB, lb_logits[0]),
                    (R_C, c[0]), (R_CCTX, c_ctx))
            for r, v in rows:
                sp.dma_start(vrow[r:r + KD, :], v.rearrange("(k p) -> k p", p=P)).then_inc(s_const, 16)
            sp.dma_start(vrow[R_ONORM:R_ONORM + 1, :], o_norm).then_inc(s_const, 16)
            sp.dma_start(brow[0:96, :], b_ada[0].rearrange("(k p) -> k p", p=P)).then_inc(s_const, 16)
            for t in range(4):
                src = crows[t] if t < 2 else xrows[t - 2]
                sp.dma_start(xin[:, t, :], src).then_inc(s_x[t], 16)
            def two(slot, dst, src):
                sp.dma_start(dst[0:64], src[0:64]).then_inc(s_raw[slot], 16)
                sp.dma_start(dst[64:P], src[64:P]).then_inc(s_raw[slot], 16)

            def load(ck):
                if ck >= RAW:
                    sp.wait_ge(s_lo, ck - RAW + 1)
                slot = ck % RAW
                dst = raw[:, slot, :]
                if ck < C_B:
                    q, k = divmod(ck, KD)
                    two(slot, dst, wada[k, :, q * CW:(q + 1) * CW])
                elif ck < C_G:
                    pr, r = divmod(ck - C_B, 16)
                    kk = 2 * (r % 8)
                    a, b = (win, win) if r < 8 else (wf[0], wf[1])
                    ca = (D if r < 8 else 0) + pr * 256
                    cb = pr * 256
                    d3 = dst.rearrange("p (k n) -> p k n", k=2)
                    sp.dma_start(d3[:, :, 0:256], a[:, kk:kk + 2, ca:ca + 256]).then_inc(s_raw[slot], 16)
                    sp.dma_start(d3[:, :, 256:512], b[:, kk:kk + 2, cb:cb + 256]).then_inc(s_raw[slot], 16)
                elif ck < C_WO:
                    u, r = divmod(ck - C_G, 8)
                    d3 = dst.rearrange("p (k n) -> p k n", k=2)
                    col = 2 * D + u * 512
                    two(slot, d3, win[:, 2 * r:2 * r + 2, col:col + 512])
                elif ck < C_FF:
                    k, half = divmod(ck - C_WO, 2)
                    two(slot, dst, wo[k, :, half * CW:(half + 1) * CW])
                elif ck < C_DN:
                    u, r = divmod(ck - C_FF, 8)
                    d3 = dst.rearrange("p (k n) -> p k n", k=2)
                    two(slot, d3, wgu[u % 2][:, 2 * r:2 * r + 2, (u // 2) * 512:(u // 2) * 512 + 512])
                else:
                    k, half = divmod(ck - C_DN, 2)
                    two(slot, dst, wdn[k, :, half * CW:(half + 1) * CW])

            for ck in range(CHUNKS):
                load(ck)
                if ck == KD:
                    sp.wait_ge(s_xe, KD)
                    sp.dma_start(xdram.rearrange("p (k t) -> p k t", k=KD), xT[:, :, T:TT]).then_inc(s_xs, 16)
                i = ck - C_B
                if 0 <= i < PADA:
                    if i >= 2:
                        sp.wait_ge(s_ac, i - 1)
                    e, k = divmod(i, KD)
                    sp.dma_start(aw[:, i % 2, :], wada[k, :, 2 * D + e * CW:2 * D + (e + 1) * CW]).then_inc(s_aw[i % 2], 16)
                if ck == C_WO:
                    sp.wait_ge(s_on, HEADS)
                    sp.wait_ge(s_xs, 16)
                    sp.dma_start(xres, xdram.rearrange("p (k t) -> p k t", k=KD)).then_inc(s_xb, 16)
            for t in range(2):
                sp.wait_ge(s_fe, 4 * (t + 1))
                sp.dma_start(orows[t], outb[:, t, :]).then_inc(s_out, 16)
            sp.wait_ge(s_out, 32)

        @block.gpsimd
        def _(pool):
            pool.wait_ge(s_at, 4)
            for e in range(8):
                if e:
                    pool.wait_ge(s_ap, e)
                for k in range(KD):
                    i = e * KD + k
                    if k == 0:
                        pool.memset(aacc[:, :], 0.0).then_inc(s_az, 1)
                        pool.wait_ge(s_az, e + 1)
                    else:
                        pool.wait_ge(s_ac, i)
                    pool.wait_ge(s_am, i + 1)
                    pool.tensor_tensor(aacc[:, :], aw[:, i % 2, :], aacc[:, :], ALU.add).then_inc(s_ac, 1)

        def halves(ap, h):
            v = ap.rearrange("p d (b n) -> p d b n", n=2 * h)
            return v[:, :, :, 0:h], v[:, :, :, h:2 * h]

        def abank(q, i):
            return (score[0:4, i, :] if q % 2 == 0 else (bank[2], ob)[i][0:4, :])

        @block.scalar
        def _(act):
            def hi(ck):
                act.wait_ge(s_raw[ck % RAW], 32 * (ck // RAW + 1))
                if ck >= SPL:
                    act.wait_ge(s_used, ck - SPL + 1)
                act.activation(whi[:, ck % SPL, :], raw[:, ck % RAW, :], ACT.Copy).then_inc(s_hi, 1)

            act.wait_ge(s_vec, 1)
            act.activation(cs[:, :, 0], vec[:, R_C:R_C + KD], ACT.Silu)
            act.activation(cs[:, :, 1], vec[:, R_CCTX:R_CCTX + KD], ACT.Silu).then_inc(s_cs, 1)
            act.preload_act_table_set(EXP_LN)
            act.wait_ge(s_cs, 1)
            act.wait_ge(s_lb, 1)
            act.activation(lbt[:, 1, :], lbt[:, 0, :], ACT.Exp).then_inc(s_lb, 1)
            act.activation(cs4[:, :, :, 0], cs[:, :, :], ACT.Copy).then_inc(s_c4, 1)

            def mod_rows(q):
                act.wait_ge(s_used, KD * (q + 1))
                if q:
                    act.wait_ge(s_at, q)
                for i in range(2):
                    act.activation(arow[:, i * 512:(i + 1) * 512], abank(q, i), ACT.Copy).then_inc(s_ar, 1)

            for k in range(KD):
                act.wait_ge(s_xe, k + 1)
                if k >= 2:
                    act.wait_ge(s_ms, k - 1)
                act.activation(sq[:, k % 2, :], xT[:, k, :], ACT.Square).then_inc(s_sq, 1)
                hi(k)
            hi(KD)
            hi(KD + 1)
            act.wait_ge(s_ms, KD)
            act.activation(rstd[:, :], bank[3][:, :], ACT.Ln, bias=eps[:, :], scale=1.0 / D).then_inc(s_rs, 1)
            act.wait_ge(s_rs, 1)
            act.activation(rstd[:, :], rstd[:, :], ACT.Exp, scale=-0.5).then_inc(s_rs, 1)
            for ck in range(KD + 2, C_B):
                hi(ck)
                if ck % KD == 2:
                    mod_rows(ck // KD - 1)
            mod_rows(3)
            for k in range(KD):
                act.wait_ge(s_a, 2 * (k + 1))
                act.activation(ahi[:, k, :], xT[:, k, :], ACT.Copy).then_inc(s_ah, 1)
                if k in (0, 1):
                    hi(C_B + k)

            UNITS = ((0, 0), (1, 0), (0, 1), (1, 1))

            def gate_exps(pr, i):
                d, h = UNITS[i]
                b = pr % 2
                K = keyq[b][:, h, 2 * d, :]
                act.wait_ge(s_zc, 4 * pr + i + 1)
                if pr >= 2 and i == 0:
                    act.wait_ge(s_em, 2 * pr - 2)
                    act.wait_ge(s_sc, 4 * (2 * pr - 2))
                if 4 * pr + i >= 2:
                    act.wait_ge(s_zy, 2 * (4 * pr + i - 1))
                act.activation(K, gates[b][:, h, d, :], ACT.Exp, scale=-1.0).then_inc(s_ze, 1)
                act.wait_ge(s_ze, 3 * (4 * pr + i) + 1)
                act.activation(zt[:, i % 2, 0, :], K, ACT.Ln, bias=1.0).then_inc(s_ze, 1)
                act.activation(zt[:, i % 2, 1, :], K, ACT.Ln, bias=1.0,
                               scale=lbv[:, 2 * pr + h:2 * pr + h + 1]).then_inc(s_ze, 1)

            def gate_sigmoid(pr, i):
                d, h = UNITS[i]
                K = keyq[pr % 2][:, h, 2 * d, :]
                act.wait_ge(s_zy, 2 * (4 * pr + i) + 1)
                act.activation(K, K, ACT.Exp, scale=-1.0).then_inc(s_zk, 1)

            def values_queries(pr):
                b = pr % 2
                act.wait_ge(s_used, C_B + 16 * pr + 8)
                if pr >= 2:
                    act.wait_ge(s_o, 2 * pr - 2)
                    act.wait_ge(s_sc, 4 * (2 * pr - 2))
                    act.wait_ge(s_xm, 2 * pr - 2)
                    act.wait_ge(s_em, 2 * pr - 2)
                for i in range(2):
                    act.activation(vals[b][:, 2 * i:2 * i + 2, :],
                                   bank[i][:, :].rearrange("p (t v) -> p t v", t=2), ACT.Copy).then_inc(s_vev, 1)
                act.activation(keyq[b][:, :, 1, T:TT], bank[2][:, :].rearrange("p (h t) -> p h t", h=2),
                               ACT.Silu).then_inc(s_qev, 1)
                act.preload_act_table_set(EXP_LN)

            def scan(j, n):
                m = n % 2
                if j == 1:
                    act.wait_ge(s_cum, n + 1)
                    if n:
                        act.wait_ge(s_tr, 2 * n)
                        act.wait_ge(s_o, n)
                        act.wait_ge(s_s2, n)
                    act.activation(xs[:, 0, 0, :], pcum[:, 0, 0:P], ACT.Exp, bias=tot[:, m, 0, 0:1], scale=-1.0)
                    act.activation(xs[:, 0, 1, :], pcum[:, 0, P:2 * P], ACT.Exp, bias=pcum[:, 0, 2 * P - 1:2 * P], scale=-1.0)
                    act.activation(xs[:, 0, 2, :], pcum[:, 0, 2 * P:3 * P], ACT.Exp, bias=pcum[:, 0, 3 * P - 1:3 * P], scale=-1.0)
                    act.activation(xs[:, 1, 0, :], pcum[:, 1, 0:P], ACT.Exp)
                    act.activation(xs[:, 1, 1, :], pcum[:, 1, P:2 * P], ACT.Exp, bias=tot[:, m, 1, 0:1])
                    act.activation(xs[:, 1, 2, :], pcum[:, 1, 3 * P:TT], ACT.Exp)
                    act.activation(xi[:, 0, :], pcum[:, 0, T:TT], ACT.Exp)
                    for t in range(2):
                        act.activation(xi[:, 1, t * P:(t + 1) * P], pcum[:, 1, T + t * P:T + (t + 1) * P], ACT.Exp,
                                       bias=tot[:, m, 1, 2 + t:3 + t], scale=-1.0)
                    act.activation(etot[:, m, 0:1], pcum[:, 0, 3 * P - 1:3 * P], ACT.Exp)
                    act.activation(etot[:, m, 1:2], tot[:, m, 1, 3:4], ACT.Exp).then_inc(s_ex, 1)
                    act.wait_ge(s_sub, 2 * n + 1)
                    act.activation(eseq[:, :, 0:3 * T], eseq[:, :, 0:3 * T], ACT.Exp).then_inc(s_el, 1)
                if j == 2:
                    act.wait_ge(s_sub, 2 * n + 2)
                    act.activation(eseq[:, :, 3 * T:NL * T], eseq[:, :, 3 * T:NL * T], ACT.Exp).then_inc(s_el, 1)
                if j == 6:
                    for d in range(2):
                        act.wait_ge(s_tr, 2 * n + d + 1)
                        act.activation(kt[:, d, :, :], (mx, ob)[d][:, 0:384].rearrange("p (j t) -> p j t", j=3),
                                       ACT.Copy).then_inc(s_kt, 1)
                if j == 7:
                    act.wait_ge(s_st, n + 1)
                    act.activation(state[:, 0, :, :], mx[:, 0:256].rearrange("p (d v) -> p d v", d=2),
                                   ACT.Copy).then_inc(s_s1, 1)
                if j == 9:
                    act.wait_ge(s_o, n + 1)
                    act.activation(osq, ob[:, 0:T], ACT.Square).then_inc(s_osq, 1)
                if j == 10:
                    act.wait_ge(s_om, n + 1)
                    if n:
                        act.wait_ge(s_on, n)
                    act.activation(rstd[:, 0:T], mx[:, 0:T], ACT.Ln, bias=eps[:, :], scale=1.0 / P).then_inc(s_ol, 1)
                    act.wait_ge(s_ol, n + 1)
                    act.activation(rstd[:, 0:T], rstd[:, 0:T], ACT.Exp, scale=-0.5).then_inc(s_or, 1)

            def gate_silu(u):
                act.wait_ge(s_used, C_G + 8 * (u + 1))
                for i in range(2):
                    if u:
                        act.wait_ge(s_y, 2 * u)
                    else:
                        act.wait_ge(s_zy, 8 * PAIRS)
                    act.activation(zt[:, i, 0, :], bank[2 * (u % 2) + i][:, :], ACT.Silu).then_inc(s_gev, 1)
                act.preload_act_table_set(EXP_LN)

            for ck, kind, u, r, tasks in positions():
                if ck >= C_B + 2:
                    hi(ck)
                i = ck - C_B - 1
                if 0 <= i < PADA:
                    act.wait_ge(s_aw[i % 2], 16 * (i // 2 + 1))
                    act.activation(aw[:, i % 2, :], aw[:, i % 2, :], ACT.Copy,
                                   scale=cs[:, i % KD, 0:1]).then_inc(s_am, 1)
                if kind == "Z" and r == 0:
                    values_queries(u)
                p = ck % 16
                if p < 3 and C_B + 16 <= ck < C_G + 3:
                    pr = (ck - C_B) // 16 - 1
                    if p > 0:
                        for i in (2 * p - 2, 2 * p - 1):
                            gate_sigmoid(pr, i)
                    if p < 2:
                        for i in (2 * p, 2 * p + 1):
                            gate_exps(pr, i)
                if kind == "G" and r == 0 and u:
                    gate_silu(u - 1)
                for j, n in tasks:
                    scan(j, n)
            gate_silu(3)

            for k in range(KD):
                act.wait_ge(s_y, 2 * (k // 4) + (k % 4) // 2 + 1)
                if k >= 2:
                    act.wait_ge(s_used, C_WO + 2 * (k - 1))
                else:
                    act.wait_ge(s_used, C_WO)
                act.activation(yhi[:, k % 2, :], oT[:, k, :], ACT.Copy).then_inc(s_yh, 1)
                hi(C_WO + 2 * k)
                hi(C_WO + 2 * k + 1)
            for k in range(KD):
                act.wait_ge(s_h, k + 1)
                if k >= 2:
                    act.wait_ge(s_hm, k - 1)
                act.activation(sq[:, k % 2, 0:T], hT[:, k, :], ACT.Square).then_inc(s_hq, 1)
            hi(C_FF)
            hi(C_FF + 1)
            act.wait_ge(s_hm, KD)
            act.activation(rstd[:, 0:T], ob[:, 0:T], ACT.Ln, bias=eps[:, :], scale=1.0 / D).then_inc(s_hr, 1)
            act.wait_ge(s_hr, 1)
            act.activation(rstd[:, 0:T], rstd[:, 0:T], ACT.Exp, scale=-0.5).then_inc(s_hr, 1)
            for k in range(KD):
                act.wait_ge(s_ht, 2 * (k + 1))
                act.activation(ahi[:, k, 0:T], zt[:, 0, k % 2, 0:T], ACT.Copy).then_inc(s_ah, 1)
            for u in range(2 * FG):
                for r in range(8):
                    ck = C_FF + 8 * u + r
                    if ck >= C_FF + 2:
                        hi(ck)
                    if r == 0 and u % 2 == 1:
                        j = u // 2
                        act.wait_ge(s_used, C_FF + 8 * u)
                        if j:
                            act.wait_ge(s_fh, 2 * j)
                        for i in range(2):
                            act.activation(sq[:, i, :], bank[i][:, :], ACT.Silu).then_inc(s_fgs, 1)
            act.preload_act_table_set(EXP_LN)
            for k in range(KF):
                act.wait_ge(s_fh, 2 * (k // 4) + (k % 4) // 2 + 1)
                if k >= 2:
                    act.wait_ge(s_used, C_DN + 2 * (k - 1))
                else:
                    act.wait_ge(s_used, C_FF)
                act.activation(yhi[:, k % 2, :], h1[:, k, :], ACT.Copy).then_inc(s_yh, 1)
                hi(C_DN + 2 * k)
                hi(C_DN + 2 * k + 1)
            for k in range(KD):
                act.wait_ge(s_fo, k + 1)
                if k >= 2:
                    act.wait_ge(s_fm, k - 1)
                act.activation(sq[:, k % 2, 0:T], hT[:, k, :], ACT.Square).then_inc(s_fq, 1)
            act.wait_ge(s_fm, KD)
            act.activation(rcol[:, 0, :], bank[1][:, 0:2], ACT.Ln, bias=eps[:, :], scale=1.0 / D).then_inc(s_fr, 1)
            act.wait_ge(s_fr, 1)
            act.activation(rcol[:, 1, :], rcol[:, 0, :], ACT.Exp, scale=-0.5).then_inc(s_fr, 1)

        def hidden(dve, j):
            dve.wait_ge(s_used, C_FF + 16 * (j + 1))
            for i in range(2):
                dve.wait_ge(s_fgs, 2 * j + i + 1)
                k = 4 * j + 2 * i
                dve.tensor_tensor(h1[:, k:k + 2, :], sq[:, i, :].rearrange("p (k t) -> p k t", k=2),
                                  bank[2 + i][:, :].rearrange("p (k t) -> p k t", k=2), ALU.mult).then_inc(s_fh, 1)

        @block.vector
        def _(dve):
            def lo(ck):
                dve.wait_ge(s_hi, ck + 1)
                dve.tensor_tensor(wlo[:, ck % SPL, :], raw[:, ck % RAW, :], whi[:, ck % SPL, :].bitcast(F32),
                                  ALU.subtract).then_inc(s_lo, 1)

            dve.memset(ones[:, :], 1.0)
            dve.memset(eps[:, :], EPS).then_inc(s_one, 1)
            dve.wait_ge(s_vecT, 1)
            dve.tensor_copy(vec[:, :], mx[:, 0:VROWS]).then_inc(s_vec, 1)
            dve.tensor_copy(bias[:, :], mx[:, 128:224]).then_inc(s_vec, 1)
            dve.wait_ge(s_vec, 2)
            lg = vec[:, R_LB:R_LB + KD]
            dve.tensor_tensor(lbt[:, 0, :], lg, lg, ALU.subtract).then_inc(s_lb, 1)
            dve.wait_ge(s_lb, 2)
            dve.reciprocal(lbt[:, 2, :], lbt[:, 1, :]).then_inc(s_lb, 1)
            dve.wait_ge(s_lb, 3)
            dve.tensor_tensor(lbt[:, 0, :], lbt[:, 1, :], lbt[:, 2, :], ALU.mult).then_inc(s_lb, 1)
            dve.wait_ge(s_lb, 4)
            dve.tensor_tensor(lbv, lbt[:, 0, :], lbt[:, 0, :], ALU.subtract).then_inc(s_lb, 1)
            dve.wait_ge(s_lb, 5)
            dve.tensor_scalar(oml[:, :], lbv, -1.0, 1.0, ALU.mult, ALU.add).then_inc(s_mod, 1)
            dve.wait_ge(s_c4, 1)
            dve.tensor_tensor(cs4[:, :, :, 1], cs[:, :, :], cs4[:, :, :, 0].bitcast(F32), ALU.subtract).then_inc(s_c4, 1)
            for k in range(KD):
                dve.wait_ge(s_xt, k + 1)
                dve.tensor_copy(xT[:, k, :], bank[k % 2][:, :]).then_inc(s_xe, 1)
                if k:
                    lo(k - 1)
            lo(KD - 1)
            lo(KD)
            lo(KD + 1)
            dve.wait_ge(s_rs, 2)
            for ck in range(KD + 2, C_B):
                lo(ck)
                k = ck - KD - 6
                if 0 <= k < KD:
                    if k == 0:
                        dve.wait_ge(s_xs, 16)
                    dve.tensor_tensor(xT[:, k, :], xT[:, k, :], rstd[:, :], ALU.mult).then_inc(s_xn, 1)
            dve.wait_ge(s_at, 4)
            am = mx[:, 0:128].rearrange("p (m k s i) -> p m k s i", m=2, s=2, i=2)
            b2 = bias[:, 0:2 * KD].rearrange("p (m k) -> p m k", m=2)
            dve.tensor_tensor(mod[:, 0:2, :], am[:, :, :, 0, 0], b2, ALU.add)
            dve.tensor_tensor(modc[:, :, :], am[:, :, :, 1, 0], b2, ALU.add).then_inc(s_mod, 1)
            dve.wait_ge(s_mod, 2)
            dve.tensor_tensor(mod[:, 0:2, :], am[:, :, :, 0, 1], mod[:, 0:2, :], ALU.add)
            dve.tensor_tensor(modc[:, :, :], am[:, :, :, 1, 1], modc[:, :, :], ALU.add).then_inc(s_mod, 1)
            dve.wait_ge(s_mod, 3)
            nm = vec[:, R_NMIX:R_NMIX + KD]
            dve.scalar_tensor_tensor(out=scl[:, 0, :], in0=modc[:, 1, :], scalar=1.0, in1=nm, op0=ALU.add,
                                     op1=ALU.mult).then_inc(s_mod, 1)
            dve.scalar_tensor_tensor(out=scl[:, 1, :], in0=mod[:, 1, :], scalar=1.0, in1=nm, op0=ALU.add,
                                     op1=ALU.mult).then_inc(s_mod, 1)
            dve.wait_ge(s_mod, 5)
            dve.wait_ge(s_xn, KD)
            for k in range(KD):
                for i, sh in enumerate((modc[:, 0, k:k + 1], mod[:, 0, k:k + 1])):
                    v = xT[:, k, i * T:(i + 1) * T]
                    dve.tensor_scalar(v, v, scl[:, i, k:k + 1], sh, ALU.mult, ALU.add).then_inc(s_a, 1)
                if k:
                    q = k - 1
                    dve.wait_ge(s_ah, q + 1)
                    dve.tensor_tensor(alo[:, q, :], xT[:, q, :], ahi[:, q, :].bitcast(F32), ALU.subtract).then_inc(s_al, 1)
                if k in (1, 2):
                    lo(C_B + k - 1)
            dve.wait_ge(s_ah, KD)
            dve.tensor_tensor(alo[:, KD - 1, :], xT[:, KD - 1, :], ahi[:, KD - 1, :].bitcast(F32),
                              ALU.subtract).then_inc(s_al, 1)

            UNITS = ((0, 0), (1, 0), (0, 1), (1, 1))

            def clip_gates(pr):
                dve.wait_ge(s_used, C_B + 16 * (pr + 1))
                if pr >= 2:
                    dve.wait_ge(s_cum, 2 * pr - 2)
                for i, (d, h) in enumerate(UNITS):
                    dve.tensor_scalar(gates[pr % 2][:, h, d, :], bank[2 * d + h][:, :], -CLIP, CLIP, ALU.max,
                                      ALU.min).then_inc(s_zc, 1)

            def log_gates(pr, i):
                d, h = UNITS[i]
                b = pr % 2
                n = 4 * pr + i
                G, K = gates[b][:, h, d, :], keyq[b][:, h, 2 * d, :]
                dve.wait_ge(s_ze, 3 * n + 3)
                dve.wait_ge(s_zc, n + 1)
                dve.tensor_tensor(K, G, zt[:, i % 2, 0, :], ALU.add).then_inc(s_zy, 1)
                dve.wait_ge(s_zy, 2 * n + 1)
                dve.tensor_tensor(G, zt[:, i % 2, 1, :], zt[:, i % 2, 0, :], ALU.subtract).then_inc(s_zy, 1)

            def keys(pr, i):
                d, h = UNITS[i]
                K = keyq[pr % 2][:, h, 2 * d, :]
                dve.wait_ge(s_zk, 4 * pr + i + 1)
                dve.tensor_scalar(K, K, oml[:, 2 * pr + h:2 * pr + h + 1], None, ALU.mult).then_inc(s_k, 1)

            def scale_queries(pr):
                dve.wait_ge(s_qev, pr + 1)
                Q = keyq[pr % 2][:, :, 1, T:TT]
                dve.tensor_scalar(Q, Q, QSCALE, None, ALU.mult).then_inc(s_qs, 1)

            def levels(n, which):
                for li in which:
                    h = HALVES[li]
                    xl, xr = halves(pcum[:, :, T:TT], h)
                    el, er = halves(ebuf[:, :, li, :], h)
                    nb = T // (2 * h)
                    r = mid_ap(h, nb)
                    dve.tensor_tensor(el, r, xl, ALU.subtract)
                    last = dve.tensor_tensor(er, xr, r, ALU.subtract)
                last.then_inc(s_sub, 1)

            def mid_ap(h, nb):
                full = pcum[:, :, T:TT]
                pstep = full.ap[0]
                return bass.AP(tensor=full.tensor, offset=full.offset + h - 1,
                               ap=[list(pstep), [TT + 1, 2], [2 * h, nb], [0, h]])

            def level_muls(n, which, last_one):
                b, hh = (n // 2) % 2, n % 2
                kq = keyq[b][:, hh, :, T:TT]
                for li in which:
                    h = HALVES[li]
                    el, er = halves(ebuf[:, :, li, :], h)
                    ml, _ = halves(kq[:, 0:2, :], h)
                    _, mr = halves(kq[:, 1:3, :], h)
                    dve.tensor_tensor(el, el, ml, ALU.mult)
                    last = dve.tensor_tensor(er, er, mr, ALU.mult)
                if last_one:
                    last.then_inc(s_em, 1)

            def place(n, step):
                d, t = divmod(step, 2)
                dve.wait_ge(s_sc, 4 * n + step + 1)
                if d == 0:
                    dve.tensor_tensor(pT[:, t, :], score[:, 1, 3 * P:4 * P], ident[:, :], ALU.mult).then_inc(s_dg, 1)
                    dve.wait_ge(s_dg, 2 * n + t + 1)
                for li, h in enumerate(HALVES):
                    h0 = h if d == 0 else 0
                    dst = pT[:, t, :].rearrange("p (b n) -> p b n", n=2 * h)[:, :, h0:h0 + h]
                    src = score[:, li // 4, (li % 4) * P:(li % 4 + 1) * P]
                    src = src.rearrange("p (b n) -> p b n", n=2 * h)[:, :, h0:h0 + h]
                    off = (d * NL + li) * 64
                    m = masks[:, off:off + 64].rearrange("p (b n) -> p b n", n=h)
                    dve.copy_predicated(dst, m, src).then_inc(s_pl, 1)
                    dve.wait_ge(s_pl, (4 * n + step) * NL + li + 1)

            def scan(j, n):
                b, hh, m = (n // 2) % 2, n % 2, n % 2
                G, KQ = gates[b], keyq[b]
                if j == 0:
                    dve.wait_ge(s_k, 4 * (n // 2) + 2 * hh + 2)
                    dve.wait_ge(s_zy, 2 * (4 * (n // 2) + 2 * hh + 2))
                    dve.wait_ge(s_qs, n // 2 + 1)
                    if n:
                        dve.wait_ge(s_ex, n)
                        dve.wait_ge(s_sub, 2 * n)
                    if n >= 2:
                        dve.wait_ge(s_s2, n - 1)
                    dve.tensor_tensor_scan(pcum[:, 0, :], keep[:, :], G[:, hh, 0, :], 0.0, ALU.mult, ALU.add)
                    g1 = G[:, hh, 1, :]
                    shifted = bass.AP(tensor=g1.tensor, offset=g1.offset - 1, ap=[list(a) for a in g1.ap])
                    dve.tensor_tensor_scan(pcum[:, 1, :], shifted, keep[:, :], 0.0, ALU.add, ALU.mult).then_inc(s_cd, 1)
                    dve.wait_ge(s_cd, n + 1)
                    dve.tensor_tensor(tot[:, m, 0, 0:1], pcum[:, 0, P - 1:P], pcum[:, 0, 2 * P - 1:2 * P], ALU.add)
                    ends = slice(P - 1, TT, P)
                    dve.tensor_tensor(tot[:, m, 1, 0:4], pcum[:, 1, ends], G[:, hh, 1, ends], ALU.add).then_inc(s_cum, 1)
                    if n:
                        dve.wait_ge(s_sc, 4 * n)
                    dve.tensor_tensor(ksum, KQ[:, hh, 0, T:TT], KQ[:, hh, 2, T:TT], ALU.add)
                    levels(n, (0, 1, 2))
                if j == 1:
                    levels(n, (3, 4, 5, 6))
                if j == 2:
                    dve.wait_ge(s_ex, n + 1)
                    dve.tensor_tensor(xs[:, 0, :, :], xs[:, 0, :, :],
                                      KQ[:, hh, 0, 0:3 * P].rearrange("p (j t) -> p j t", j=3), ALU.mult)
                    dve.tensor_tensor(xs[:, 1, 0:2, :], xs[:, 1, 0:2, :],
                                      KQ[:, hh, 2, 0:2 * P].rearrange("p (j t) -> p j t", j=2), ALU.mult)
                    dve.tensor_tensor(xs[:, 1, 2, :], xs[:, 1, 2, :], KQ[:, hh, 2, 3 * P:TT], ALU.mult)
                    for d in range(2):
                        last = dve.tensor_tensor(xi[:, d, :], xi[:, d, :], KQ[:, hh, 1, T:TT], ALU.mult)
                    last.then_inc(s_xm, 1)
                    dve.wait_ge(s_el, 2 * n + 1)
                    level_muls(n, (0, 1), False)
                if j == 3:
                    dve.wait_ge(s_el, 2 * n + 2)
                    level_muls(n, (2, 3, 4, 5, 6), True)
                if j == 7:
                    dve.wait_ge(s_s1, n + 1)
                    for d in range(2):
                        last = dve.scalar_tensor_tensor(out=state[:, 1, d, :], in0=state[:, 0, d, :],
                                                        scalar=etot[:, m, d:d + 1],
                                                        in1=mx[:, 256 + d * P:384 + d * P], op0=ALU.mult, op1=ALU.add)
                    last.then_inc(s_s2, 1)
                if 5 <= j <= 8:
                    if j == 5 and n:
                        dve.wait_ge(s_o, n)
                    place(n, j - 5)
                if j == 11:
                    dve.wait_ge(s_or, n + 1)
                    dve.scalar_tensor_tensor(out=oT[:, n, :], in0=ob[:, 0:T], scalar=vec[:, R_ONORM:R_ONORM + 1],
                                             in1=rstd[:, 0:T], op0=ALU.mult, op1=ALU.mult).then_inc(s_on, 1)

            def gate_outputs(u):
                for i in range(2):
                    dve.wait_ge(s_gev, 2 * u + i + 1)
                    dve.wait_ge(s_on, 4 * u + 2 * i + 2)
                    v = oT[:, 4 * u + 2 * i:4 * u + 2 * i + 2, :]
                    dve.tensor_tensor(v, v, zt[:, i, 0, :].rearrange("p (k t) -> p k t", k=2), ALU.mult).then_inc(s_y, 1)

            def add_modulation(e):
                dve.wait_ge(s_ap, e + 1)
                v = mod[:, 2 + e // 2, (e % 2) * 8:(e % 2) * 8 + 8]
                o = 2 * KD + 8 * e
                dve.tensor_tensor(v, bank[3][:, 0:8], bias[:, o:o + 8], ALU.add).then_inc(s_av, 1)

            for ck, kind, u, r, tasks in positions():
                if ck >= C_B + 2:
                    lo(ck)
                if kind == "Z" and r == 1:
                    scale_queries(u)
                p = ck % 16
                if p < 4 and C_B + 16 <= ck < C_G + 4:
                    pr = (ck - C_B) // 16 - 1
                    if p == 0:
                        clip_gates(pr)
                    if p in (1, 2):
                        for i in (2 * p - 2, 2 * p - 1):
                            log_gates(pr, i)
                    if p in (2, 3):
                        for i in (2 * p - 4, 2 * p - 3):
                            keys(pr, i)
                if kind == "G" and r == 1 and u:
                    gate_outputs(u - 1)
                if ADA_AT(ck) is not None:
                    add_modulation(ADA_AT(ck))
                for j, n in tasks:
                    scan(j, n)
            gate_outputs(3)

            for k in range(KD):
                dve.wait_ge(s_yh, k + 1)
                dve.wait_ge(s_y, 2 * (k // 4) + (k % 4) // 2 + 1)
                dve.tensor_tensor(ylo[:, k % 2, :], oT[:, k, :], yhi[:, k % 2, :].bitcast(F32), ALU.subtract).then_inc(s_yl, 1)
                lo(C_WO + 2 * k)
                lo(C_WO + 2 * k + 1)
            dve.wait_ge(s_av, 8)
            dve.scalar_tensor_tensor(out=sclf[:, :], in0=mod[:, 4, :], scalar=1.0, in1=vec[:, R_NFFN:R_NFFN + KD],
                                     op0=ALU.add, op1=ALU.mult).then_inc(s_mod, 1)
            dve.wait_ge(s_used, C_FF)
            dve.wait_ge(s_xb, 16)
            for k in range(KD):
                dve.scalar_tensor_tensor(out=hT[:, k, :], in0=all8[k // 2][:, (k % 2) * T:(k % 2) * T + T],
                                         scalar=mod[:, 2, k:k + 1], in1=xres[:, k, :], op0=ALU.mult,
                                         op1=ALU.add).then_inc(s_h, 1)
            lo(C_FF)
            lo(C_FF + 1)
            dve.wait_ge(s_hr, 2)
            dve.wait_ge(s_mod, 6)
            for k in range(KD):
                if k >= 2:
                    dve.wait_ge(s_al, KD + k - 1)
                t, a = zt[:, 1, k % 2, 0:T], zt[:, 0, k % 2, 0:T]
                dve.wait_ge(s_h, k + 1)
                dve.tensor_tensor(t, hT[:, k, :], rstd[:, 0:T], ALU.mult).then_inc(s_ht, 1)
                dve.wait_ge(s_ht, 2 * k + 1)
                dve.tensor_scalar(a, t, sclf[:, k:k + 1], mod[:, 3, k:k + 1], ALU.mult, ALU.add).then_inc(s_ht, 1)
                dve.wait_ge(s_ah, KD + k + 1)
                dve.wait_ge(s_ht, 2 * k + 2)
                dve.tensor_tensor(alo[:, k, 0:T], a, ahi[:, k, 0:T].bitcast(F32), ALU.subtract).then_inc(s_al, 1)
            for u in range(2 * FG):
                for r in range(8):
                    ck = C_FF + 8 * u + r
                    if ck >= C_FF + 2:
                        lo(ck)
                    if r == 0 and u % 2 == 0 and u:
                        hidden(dve, u // 2 - 1)
            hidden(dve, FG - 1)
            for k in range(KF):
                dve.wait_ge(s_yh, KD + k + 1)
                dve.wait_ge(s_fh, 2 * (k // 4) + (k % 4) // 2 + 1)
                dve.tensor_tensor(ylo[:, k % 2, :], h1[:, k, :], yhi[:, k % 2, :].bitcast(F32), ALU.subtract).then_inc(s_yl, 1)
                lo(C_DN + 2 * k)
                lo(C_DN + 2 * k + 1)
            dve.wait_ge(s_used, CHUNKS)
            for k in range(KD):
                dve.scalar_tensor_tensor(out=hT[:, k, :], in0=all8[k // 2][:, (k % 2) * T:(k % 2) * T + T],
                                         scalar=mod[:, 5, k:k + 1], in1=hT[:, k, :], op0=ALU.mult,
                                         op1=ALU.add).then_inc(s_fo, 1)
            for k in range(KD):
                dve.wait_ge(s_fq, k + 1)
                dve.wait_ge(s_fo, k + 1)
                dve.tensor_scalar(hT[:, k, :], hT[:, k, :], vec[:, R_FIN + k:R_FIN + k + 1], None,
                                  ALU.mult).then_inc(s_fs, 1)
            dve.wait_ge(s_fr, 2)
            for t in range(2):
                for q in range(4):
                    i = 4 * t + q
                    dve.wait_ge(s_ft, i + 1)
                    dve.tensor_scalar(outb[:, t, q * 512:(q + 1) * 512], all8[2 + i % 6], rcol[:, 1, t:t + 1], None,
                                      ALU.mult).then_inc(s_fe, 1)

        def mean_square(pe, k):
            pe.wait_ge(s_one, 1)
            pe.wait_ge(s_sq, k + 1)
            pe.matmul(bank[3][:, :], ones[:, :], sq[:, k % 2, :], start=(k == 0), stop=(k == KD - 1)).then_inc(s_ms, 1)


        def mod_sum(pe, ck):
            q, k = divmod(ck, KD)
            pe.wait_ge(s_lo, ck + 1)
            if ck == 0:
                pe.wait_ge(s_c4, 2)
            if q >= 2 and k == 0:
                pe.wait_ge(s_ar, 2 * (q - 1))
            cc = cs4[:, k, :, :].rearrange("p s i -> p (s i)")
            for i in range(2):
                pe.matmul(abank(q, i), cc, whi[:, ck % SPL, i * 512:(i + 1) * 512], start=(k == 0), stop=False)
                last = pe.matmul(abank(q, i), cc, wlo[:, ck % SPL, i * 512:(i + 1) * 512], start=False, stop=(k == KD - 1))
            last.then_inc(s_used, 1)

        def turn_rows(pe, q):
            pe.wait_ge(s_ar, 2 * (q + 1))
            if q == 0:
                pe.wait_ge(s_vec, 2)
            for f in range(8):
                o = 32 * q + 4 * f
                last = pe.transpose(mx[:, o:o + 4], arow[:, f * P:(f + 1) * P], ident[0:4, 0:4])
            last.then_inc(s_at, 1)

        @block.tensor
        def _(pe):
            pe.wait_ge(s_const, 16 * 11)
            pe.transpose(mx[:, 0:VROWS], vrow[0:VROWS, :], ident[0:VROWS, 0:VROWS])
            pe.transpose(mx[:, 128:224], brow[0:96, :], ident[0:96, 0:96]).then_inc(s_vecT, 1)
            for t in range(4):
                pe.wait_ge(s_x[t], 16)
            for k in range(KD):
                if k >= 2:
                    pe.wait_ge(s_xe, k - 1)
                for t in range(4):
                    last = pe.transpose(bank[k % 2][:, t * P:(t + 1) * P], xin[:, t, k * P:(k + 1) * P], ident[:, :])
                last.then_inc(s_xt, 1)
                if k >= 1:
                    mean_square(pe, k - 1)
                    mod_sum(pe, k - 1)
            mean_square(pe, KD - 1)
            for i in range(KD - 1, C_B):
                mod_sum(pe, i)
                if i % KD == 1 and i > KD:
                    turn_rows(pe, i // KD - 1)
            turn_rows(pe, 3)

            def three(dst, w, wl, ah, al, start, stop):
                pe.matmul(dst, w, ah, start=start, stop=False, skip_group_check=True)
                pe.matmul(dst, w, al, start=False, stop=False, skip_group_check=True)
                return pe.matmul(dst, wl, ah, start=False, stop=stop, skip_group_check=True)

            def chunk(ck, kind, r, u=0):
                s = ck % SPL
                for a in range(2):
                    k = 2 * r + a
                    first, end = k == 0, k == KD - 1
                    if ck < C_B + 8 and kind == "VQ":
                        pe.wait_ge(s_al, k + 1)
                    if kind == "FF" and u == 0:
                        pe.wait_ge(s_al, KD + k + 1)
                    if kind == "VQ":
                        for t in range(4):
                            dst = bank[t // 2][:, (t % 2) * T:(t % 2 + 1) * T]
                            o = slice(512 * a, 512 * a + 256)
                            tk = slice(t * P, (t + 1) * P)
                            st = first and t % 2 == 0
                            pe.matmul(dst, ahi[:, k, tk], whi[:, s, o], start=st, stop=False, skip_group_check=True)
                            pe.matmul(dst, ahi[:, k, tk], wlo[:, s, o], start=False, stop=False, skip_group_check=True)
                            pe.matmul(dst, alo[:, k, tk], whi[:, s, o], start=False, stop=end, skip_group_check=True)
                        for f in range(2):
                            o = slice(512 * a + 256 + f * P, 512 * a + 256 + (f + 1) * P)
                            last = three(bank[2][:, f * T:(f + 1) * T], whi[:, s, o], wlo[:, s, o], ahi[:, k, T:TT],
                                         alo[:, k, T:TT], first and f == 0, end)
                    elif kind == "Z":
                        for f in range(4):
                            if first:
                                if f == 0:
                                    pass
                            o = slice(512 * a + f * P, 512 * a + (f + 1) * P)
                            last = three(bank[f][:, :], whi[:, s, o], wlo[:, s, o], ahi[:, k, :], alo[:, k, :], first, end)
                    else:
                        tk = slice(T, TT) if kind == "G" else slice(0, T)
                        bb = 2 * (u % 2)
                        for f in range(4):
                            o = slice(512 * a + f * P, 512 * a + (f + 1) * P)
                            last = three(bank[bb + f // 2][:, (f % 2) * T:(f % 2 + 1) * T], whi[:, s, o], wlo[:, s, o],
                                         ahi[:, k, tk], alo[:, k, tk], first and f % 2 == 0, end)
                last.then_inc(s_used, 1)

            def wide(ck, i, half, k_end):
                s = ck % SPL
                for f in range(8):
                    ft = 8 * half + f
                    o = slice(f * P, (f + 1) * P)
                    last = three(all8[ft // 2][:, (ft % 2) * T:(ft % 2 + 1) * T], whi[:, s, o], wlo[:, s, o],
                                 yhi[:, i % 2, :], ylo[:, i % 2, :], i == 0 and ft % 2 == 0, i == k_end)
                last.then_inc(s_used, 1)

            def scan(j, n):
                b, hh = (n // 2) % 2, n % 2
                KQ = keyq[b]
                V = vals[b][:, :, hh * P:(hh + 1) * P]
                if j == 5:
                    pe.wait_ge(s_xm, n + 1)
                    for d in range(2):
                        if n:
                            pe.wait_ge(s_on, n)
                        for i in range(3):
                            last = pe.transpose((mx, ob)[d][:, i * P:(i + 1) * P], xs[:, d, i, :], ident[:, :])
                        last.then_inc(s_tr, 1)
                if j == 6:
                    pe.wait_ge(s_kt, 2 * n + 2)
                    pe.wait_ge(s_vev, 2 * (n // 2) + 2)
                    for d in range(2):
                        for t in range(2):
                            pe.matmul(mx[:, d * P:(d + 1) * P], kt[:, d, t, :], V[:, t, :], start=(t == 0), stop=(t == 1))
                    for d in range(2):
                        last = pe.matmul(mx[:, 256 + d * P:384 + d * P], kt[:, d, 2, :], V[:, 2 + d, :], start=True, stop=True)
                    last.then_inc(s_st, 1)
                if 4 <= j <= 7:
                    d, t = divmod(j - 4, 2)
                    pe.wait_ge(s_em, n + 1)
                    if n or j > 4:
                        pe.wait_ge(s_pl, (4 * n + j - 4) * NL)
                    for li in range(NL):
                        e = ebuf[:, d, li, t * P:(t + 1) * P]
                        last = pe.matmul(score[:, li // 4, (li % 4) * P:(li % 4 + 1) * P], e, e, start=True, stop=True)
                    if d == 0:
                        last = pe.matmul(score[:, 1, 3 * P:4 * P], ksum[:, t * P:(t + 1) * P],
                                         KQ[:, hh, 1, T + t * P:T + (t + 1) * P], start=True, stop=True)
                    last.then_inc(s_sc, 1)
                if j == 8:
                    pe.wait_ge(s_pl, (4 * n + 4) * NL)
                    pe.wait_ge(s_s2, n + 1)
                    for t in range(2):
                        o = ob[:, t * P:(t + 1) * P]
                        pe.matmul(o, V[:, 2 + t, :], pT[:, t, :], start=True, stop=False)
                        pe.matmul(o, state[:, t, 0, :], xi[:, 0, t * P:(t + 1) * P], start=False, stop=False)
                        last = pe.matmul(o, state[:, 1 - t, 1, :], xi[:, 1, t * P:(t + 1) * P], start=False, stop=True)
                    last.then_inc(s_o, 1)
                if j == 9:
                    pe.wait_ge(s_osq, n + 1)
                    pe.matmul(mx[:, 0:T], ones[:, :], osq, start=True, stop=True).then_inc(s_om, 1)

            def sum_modulation(e):
                pe.wait_ge(s_ac, KD * (e + 1))
                for f in range(8):
                    last = pe.matmul(bank[3][:, f:f + 1], aacc[:, f * P:(f + 1) * P], ones[:, 0:1], start=True, stop=True)
                last.then_inc(s_ap, 1)

            for ck, kind, u, r, tasks in positions():
                if kind == "VQ" and r == 0 and u:
                    pe.wait_ge(s_zc, 4 * u)
                if kind == "Z" and r == 0:
                    pe.wait_ge(s_vev, 2 * (u + 1))
                    pe.wait_ge(s_qev, u + 1)
                    if u:
                        pe.wait_ge(s_av, u)
                if kind == "G" and r == 0:
                    if u == 0:
                        pe.wait_ge(s_zc, 4 * PAIRS)
                    elif u >= 2:
                        pe.wait_ge(s_gev, 2 * (u - 1))
                    if u == 1:
                        pe.wait_ge(s_av, 8)
                pe.wait_ge(s_lo, ck + 1)
                chunk(ck, kind, r, u)
                for j, n in tasks:
                    scan(j, n)
                if SUM_AT(ck) is not None:
                    sum_modulation(SUM_AT(ck))
            pe.wait_ge(s_on, HEADS)
            pe.wait_ge(s_gev, 8)
            for k in range(KD):
                pe.wait_ge(s_yl, k + 1)
                for half in range(2):
                    ck = C_WO + 2 * k + half
                    pe.wait_ge(s_lo, ck + 1)
                    wide(ck, k, half, KD - 1)
            for k in range(KD):
                pe.wait_ge(s_hq, k + 1)
                if k == 0:
                    pe.wait_ge(s_h, KD)
                pe.matmul(ob[:, 0:T], ones[:, :], sq[:, k % 2, 0:T], start=(k == 0), stop=(k == KD - 1)).then_inc(s_hm, 1)
            for u in range(2 * FG):
                j = u // 2
                if j:
                    if u % 2 == 0:
                        pe.wait_ge(s_fgs, 2 * j)
                    else:
                        pe.wait_ge(s_fh, 2 * j)
                for r in range(8):
                    ck = C_FF + 8 * u + r
                    pe.wait_ge(s_lo, ck + 1)
                    chunk(ck, "FF", r, u)
            pe.wait_ge(s_fh, 2 * FG)
            pe.wait_ge(s_hr, 1)
            for k in range(KF):
                pe.wait_ge(s_yl, KD + k + 1)
                for half in range(2):
                    ck = C_DN + 2 * k + half
                    pe.wait_ge(s_lo, ck + 1)
                    wide(ck, k, half, KF - 1)
            for k in range(KD):
                pe.wait_ge(s_fq, k + 1)
                if k == 0:
                    pe.wait_ge(s_fo, KD)
                for t in range(2):
                    last = pe.matmul(bank[1][:, t:t + 1], sq[:, k % 2, t * P:(t + 1) * P], ones[:, 0:1],
                                     start=(k == 0 and t == 0), stop=(k == KD - 1), skip_group_check=True)
                last.then_inc(s_fm, 1)
            for t in range(2):
                for q in range(4):
                    i = 4 * t + q
                    if i >= 6:
                        pe.wait_ge(s_fe, i - 5)
                    for f in range(4):
                        k = 4 * q + f
                        pe.wait_ge(s_fs, k + 1)
                        last = pe.transpose(all8[2 + i % 6][:, f * P:(f + 1) * P], hT[:, k, t * P:(t + 1) * P], ident[:, :])
                    last.then_inc(s_ft, 1)

def SUM_AT(ck):
    e, p = divmod(ck - C_B, 16)
    return e - 1 if p == 1 and 1 <= e <= 8 and ck < C_G + 16 else None


def ADA_AT(ck):
    e, p = divmod(ck - C_B, 16)
    return e - 1 if p == 2 and 1 <= e <= 8 and ck < C_G + 16 else None


def shape_constants():
    ident = np.eye(P, dtype=np.float32)
    keep = np.ones((P, TT), np.float32)
    keep[:, ::P] = 0.0
    masks = np.zeros((P, 2, NL, 64), np.uint32)
    s = np.arange(P)[:, None]
    j = np.arange(64)[None, :]
    for li, h in enumerate(HALVES):
        for d in range(2):
            t = (j // h) * 2 * h + j % h + (h if d == 0 else 0)
            same = s // (2 * h) == t // (2 * h)
            left = s % (2 * h) < h
            masks[:, d, li, :] = same & (left if d == 0 else ~left)
    return ident, keep, masks.reshape(P, 2 * NL * 64)


_INS = ["x", "c", "ctx", "c_ctx", "w_ada", "b_ada", "norm_mix", "norm_ffn", "hg_lb_logits", "hg_w_in", "hg_w_f",
        "hg_o_norm", "hg_w_o", "ffn_w_gate", "ffn_w_up", "ffn_w_down", "final_norm"]


def kernel(**inputs):
    import numpy as _np
    import concourse.bacc as _bacc
    from concourse import mybir as _mybir
    from concourse.bass_utils import run_bass_kernel_spmd as _run

    nc = _bacc.Bacc("TRN2", target_bir_lowering=False, num_devices=1, dynamic_dma_scratch_size=1024)
    arrays, args = {}, []
    ident, keep, masks = shape_constants()
    named = [(n, _np.ascontiguousarray(inputs[n])) for n in _INS]
    named += [("ident", ident), ("keep", keep), ("masks", masks)]
    for name, a in named:
        arrays[f"in_{name}_dram"] = a
        args.append(nc.dram_tensor(f"in_{name}_dram", a.shape, _mybir.dt.from_np(a.dtype), kind="ExternalInput").ap())
    args.append(nc.dram_tensor("out_0_dram", (1, T, D), _mybir.dt.float32, kind="ExternalOutput").ap())
    build(nc, *args)
    r = _run(nc, [arrays], core_ids=[0])
    return r.results[0]["out_0_dram"]
```

```python
from contextlib import ExitStack

import numpy as np

import concourse.bass as bass
from concourse import mybir

F32 = mybir.dt.float32
F32R = mybir.dt.float32r
U32 = mybir.dt.uint32
ALU = mybir.AluOpType
ACT = mybir.ActivationFunctionType
EXP_LN = "natural_log_exp_and_others"

P = 128
D = 2048
T = 256
TT = 2 * T
KD = D // P
HEADS = 16
PAIRS = HEADS // 2
GROUPS = PAIRS // 2
HALVES = [64, 32, 16, 8, 4, 2, 1]
NL = len(HALVES)
FF = 5632
KF = FF // P
FG = FF // 512
EPS = 1e-6
CLIP = 30.0
QSCALE = float(P) ** -0.5

CW = 1024
RAW = 4
SPL = 2
BODY = 32
C_B = KD * 4
C_G = C_B + GROUPS * BODY
C_WO = C_G + 4 * 8
C_FF = C_WO + KD * 2
C_DN = C_FF + FG * 16
CHUNKS = C_DN + KF * 2
PADA = 8 * KD

R_NMIX, R_NFFN, R_FIN, R_LB, R_C, R_CCTX, R_ONORM = 0, 16, 32, 48, 64, 80, 96
VROWS = 97


def head_slots():
    return [(-11, -4), (-3, -3), (5, -2), (13, -1), (21, 0), (29, 1)]


def tasks_at(p, groups=True):
    return [(p - s, off) for s, off in head_slots() if 0 <= p - s <= 12]


def tasks_tail(p):
    out = []
    for s, head, stretched in ((-11, HEADS - 4, False), (-3, HEADS - 3, False), (5, HEADS - 2, True), (14, HEADS - 1, True)):
        for j in range(13):
            at = s + (6 * j) // 5 if stretched else s + j
            if at == p:
                out.append((j, head))
    return out


def positions():
    for g in range(GROUPS):
        for p in range(BODY):
            kind = "Z" if p % 16 >= 8 else "VQ"
            tasks = [(j, 4 * g + off) for j, off in tasks_at(p) if 4 * g + off >= 0]
            yield C_B + g * BODY + p, kind, 2 * g + p // 16, p % 8, tasks
    for p in range(32):
        yield C_G + p, "G", p // 8, p % 8, tasks_tail(p)


def build(nc, x, c, ctx, c_ctx, w_ada, b_ada, norm_mix, norm_ffn, lb_logits, w_in, w_f, o_norm, w_o,
          w_gate, w_up, w_down, final_norm, ident_in, keep_in, masks_in, out):
    xrows = x.rearrange("b (t p) d -> (b t) p d", p=P)
    crows = ctx.rearrange("b (t p) d -> (b t) p d", p=P)
    orows = out.rearrange("b (t p) d -> (b t) p d", p=P)
    wada = w_ada[0].rearrange("(k p) n -> k p n", p=P)
    win = w_in[0].rearrange("(k p) n -> p k n", p=P)
    wf = [w_f[0, d].rearrange("(k p) n -> p k n", p=P) for d in range(2)]
    wo = w_o[0].rearrange("(k p) n -> k p n", p=P)
    wgu = [w[0].rearrange("(k p) n -> p k n", p=P) for w in (w_gate, w_up)]
    wdn = w_down[0].rearrange("(k p) n -> k p n", p=P)

    stack = ExitStack()
    with stack:
        def sb(name, shape, dt=F32):
            return stack.enter_context(nc.sbuf_tensor(name, shape, dt))

        def sem(name):
            return stack.enter_context(nc.semaphore(name))

        raw = sb("raw", [P, RAW, CW])
        whi = sb("whi", [P, SPL, CW], F32R)
        wlo = sb("wlo", [P, SPL, CW], F32R)
        ahi = sb("ahi", [P, KD, TT], F32R)
        alo = sb("alo", [P, KD, TT], F32R)
        arena = sb("arena", [P, 2 * 6144])
        xin = arena[:, 0:4 * D].rearrange("p (t d) -> p t d", t=4)
        h1 = arena[:, 0:KF * T].rearrange("p (k t) -> p k t", k=KF)
        outb = arena[:, 0:2 * D].rearrange("p (t d) -> p t d", t=2)
        pair = [arena[:, b * 6144:(b + 1) * 6144] for b in range(2)]
        gates = [a[:, 0:2048].rearrange("p (h d t) -> p h d t", h=2, d=2) for a in pair]
        keyq = [a[:, 2048:5120].rearrange("p (h s t) -> p h s t", h=2, s=3) for a in pair]
        vals = [a[:, 5120:6144].rearrange("p (t v) -> p t v", t=4) for a in pair]
        work = sb("work", [P, 4096 + 7680])
        oT = work[:, 0:4096].rearrange("p (k t) -> p k t", k=KD)
        hT = oT
        xT = work[:, 0:KD * TT].rearrange("p (k t) -> p k t", k=KD)
        ebuf = work[:, 4096:4096 + 3584].rearrange("p (d l t) -> p d l t", d=2, l=NL)
        eseq = work[:, 4096:4096 + 3584].rearrange("p (d n) -> p d n", d=2)
        pcum = work[:, 7680:8704].rearrange("p (d t) -> p d t", d=2)
        xs = work[:, 8704:9472].rearrange("p (d j t) -> p d j t", d=2, j=3)
        xi = work[:, 9472:9984].rearrange("p (d t) -> p d t", d=2)
        kt = work[:, 9984:10752].rearrange("p (d j t) -> p d j t", d=2, j=3)
        state = work[:, 10752:11264].rearrange("p (o d v) -> p o d v", o=2, d=2)
        pT = work[:, 11264:11520].rearrange("p (t n) -> p t n", t=2)
        ksum = work[:, 11520:11776]
        xres = work[:, 4096:8192].rearrange("p (k t) -> p k t", k=KD)

        rstd = sb("rstd", [P, TT])
        zt = sb("zt", [P, 2, 2, TT])
        sq = zt[:, :, 0, :]
        osq = rstd[:, T:TT]
        fsum = rstd[0:1, 0:T]
        aw = sb("aw", [P, 2, CW])
        aacc = sb("aacc", [P, CW])
        yhi = ahi[:, 0:2, T:TT]
        ylo = alo[:, 0:2, T:TT]
        ident = sb("ident", [P, P])
        ones = sb("ones", [P, P])
        keep = sb("keep", [P, TT])
        masks = sb("masks", [P, 2 * NL * 64], U32)
        vrow = arena[:, 4 * D:4 * D + P]
        brow = arena[:, 4 * D + P:4 * D + 2 * P]
        vec = sb("vec", [P, VROWS])
        bias = sb("bias", [P, 96])
        eps = sb("eps", [P, 1])
        cs = sb("cs", [P, KD, 2])
        cs4 = sb("cs4", [P, KD, 2, 2], F32R)
        mod = sb("mod", [P, 6, KD])
        modc = sb("modc", [P, 2, KD])
        arow = aacc[0:4, :]
        scl = sb("scl", [P, 2, KD])
        sclf = sb("sclf", [P, KD])
        lbt = sb("lbt", [P, 4, KD])
        lbv = lbt[:, 3, :]
        oml = sb("oml", [P, KD])
        tot = sb("tot", [P, 2, 2, 8])
        etot = sb("etot", [P, 2, 2])
        rcol = sb("rcol", [P, 2, 2])
        xdram = nc.dram_tensor("x_features", [P, KD * T], F32, kind="Internal").ap()

        bank = [stack.enter_context(nc.psum_tensor(f"bank{i}", [P, 512], F32)) for i in range(4)]
        score = stack.enter_context(nc.psum_tensor("score", [P, 2, 512], F32))
        mx = stack.enter_context(nc.psum_tensor("mx", [P, 512], F32))
        ob = stack.enter_context(nc.psum_tensor("ob", [P, 512], F32))
        all8 = [b[:, :] for b in bank] + [score[:, 0, :], score[:, 1, :], mx[:, :], ob[:, :]]

        s_const = sem("const_in")
        s_x = [sem(f"x_in{t}") for t in range(4)]
        s_vecT = sem("vectors_turned")
        s_vec = sem("vectors_ready")
        s_one = sem("ones_ready")
        s_cs = sem("silu_c_ready")
        s_lb = sem("lower_bound_steps")
        s_c4 = sem("silu_c_split")
        s_ar = sem("mod_rows_ready")
        s_at = sem("mod_rows_turned")
        s_xt = sem("x_turned")
        s_xe = sem("x_evacuated")
        s_sq = sem("x_squared")
        s_ms = sem("x_mean_square")
        s_rs = sem("x_rstd")
        s_xs = sem("x_stored")
        s_xn = sem("x_normed")
        s_mod = sem("mod_steps")
        s_ah = sem("a_hi")
        s_al = sem("a_lo")
        s_raw = [sem(f"raw_in{i}") for i in range(RAW)]
        s_hi = sem("hi_ready")
        s_lo = sem("lo_ready")
        s_used = sem("chunk_used")
        s_aw = [sem(f"aw_in{i}") for i in range(2)]
        s_az = sem("ada_cleared")
        s_am = sem("ada_products")
        s_ac = sem("ada_accumulated")
        s_ap = sem("ada_summed")
        s_av = sem("ada_evacuated")
        s_vev = sem("v_evacuated")
        s_qev = sem("q_evacuated")
        s_qs = sem("q_scaled")
        s_zc = sem("z_clipped")
        s_ze = sem("z_exps")
        s_zy = sem("z_log_f")
        s_zk = sem("z_sigmoid")
        s_k = sem("keys_ready")
        s_cd = sem("cumulated")
        s_cum = sem("totals_ready")
        s_sub = sem("exponents")
        s_ex = sem("state_exps")
        s_el = sem("level_exps")
        s_xm = sem("state_operands")
        s_em = sem("level_operands")
        s_tr = sem("keys_turned")
        s_kt = sem("turned_keys_ready")
        s_st = sem("states_summed")
        s_s1 = sem("first_state_ready")
        s_s2 = sem("second_state_ready")
        s_sc = sem("scores_ready")
        s_dg = sem("diagonal_placed")
        s_pl = sem("scores_placed")
        s_o = sem("outputs_ready")
        s_osq = sem("outputs_squared")
        s_om = sem("outputs_mean_square")
        s_ol = sem("outputs_ln")
        s_or = sem("outputs_rstd")
        s_on = sem("outputs_normed")
        s_gev = sem("gate_evacuated")
        s_y = sem("y_gated")
        s_yh = sem("y_hi")
        s_yl = sem("y_lo")
        s_wo = sem("wo_summed")
        s_xb = sem("x_back")
        s_h = sem("h_ready")
        s_hq = sem("h_squared")
        s_hm = sem("h_mean_square")
        s_hr = sem("h_rstd")
        s_ht = sem("h_scaled")
        s_fa = sem("ffn_in")
        s_fg = sem("ffn_gate")
        s_fgs = sem("ffn_gate_silu")
        s_fh = sem("ffn_hidden")
        s_dn = sem("down_summed")
        s_fo = sem("final_h")
        s_fq = sem("final_squared")
        s_fm = sem("final_mean_square")
        s_fr = sem("final_rstd")
        s_fs = sem("final_scaled")
        s_ft = sem("final_turned")
        s_fe = sem("final_evacuated")
        s_feo = sem("final_evacuated_by_scalar")
        s_fe1 = sem("final_sums_evacuated")
        s_out = sem("out_stored")

        block = stack.enter_context(nc.Block())

        @block.sync
        def _(sp):
            for dst, src in ((ident, ident_in), (keep, keep_in), (masks, masks_in)):
                sp.dma_start(dst[:, :], src).then_inc(s_const, 16)
            rows = ((R_NMIX, norm_mix[0]), (R_NFFN, norm_ffn[0]), (R_FIN, final_norm), (R_LB, lb_logits[0]),
                    (R_C, c[0]), (R_CCTX, c_ctx))
            for r, v in rows:
                sp.dma_start(vrow[r:r + KD, :], v.rearrange("(k p) -> k p", p=P)).then_inc(s_const, 16)
            sp.dma_start(vrow[R_ONORM:R_ONORM + 1, :], o_norm).then_inc(s_const, 16)
            sp.dma_start(brow[0:96, :], b_ada[0].rearrange("(k p) -> k p", p=P)).then_inc(s_const, 16)
            for t in range(4):
                src = crows[t] if t < 2 else xrows[t - 2]
                sp.dma_start(xin[:, t, :], src).then_inc(s_x[t], 16)
            def two(slot, dst, src):
                sp.dma_start(dst[0:64], src[0:64]).then_inc(s_raw[slot], 16)
                sp.dma_start(dst[64:P], src[64:P]).then_inc(s_raw[slot], 16)

            def load(ck):
                if ck >= RAW:
                    sp.wait_ge(s_lo, ck - RAW + 1)
                slot = ck % RAW
                dst = raw[:, slot, :]
                if ck < C_B:
                    q, k = divmod(ck, KD)
                    col = (q + 2) % 4 * CW
                    two(slot, dst, wada[k, :, col:col + CW])
                elif ck < C_G:
                    pr, r = divmod(ck - C_B, 16)
                    kk = 2 * (r % 8)
                    a, b = (win, win) if r < 8 else (wf[0], wf[1])
                    ca = (D if r < 8 else 0) + pr * 256
                    cb = pr * 256
                    d3 = dst.rearrange("p (k n) -> p k n", k=2)
                    sp.dma_start(d3[:, :, 0:256], a[:, kk:kk + 2, ca:ca + 256]).then_inc(s_raw[slot], 16)
                    sp.dma_start(d3[:, :, 256:512], b[:, kk:kk + 2, cb:cb + 256]).then_inc(s_raw[slot], 16)
                elif ck < C_WO:
                    u, r = divmod(ck - C_G, 8)
                    d3 = dst.rearrange("p (k n) -> p k n", k=2)
                    col = 2 * D + u * 512
                    two(slot, d3, win[:, 2 * r:2 * r + 2, col:col + 512])
                elif ck < C_FF:
                    k, half = divmod(ck - C_WO, 2)
                    two(slot, dst, wo[k, :, half * CW:(half + 1) * CW])
                elif ck < C_DN:
                    u, r = divmod(ck - C_FF, 8)
                    d3 = dst.rearrange("p (k n) -> p k n", k=2)
                    two(slot, d3, wgu[u % 2][:, 2 * r:2 * r + 2, (u // 2) * 512:(u // 2) * 512 + 512])
                else:
                    k, half = divmod(ck - C_DN, 2)
                    two(slot, dst, wdn[k, :, half * CW:(half + 1) * CW])

            for ck in range(CHUNKS):
                load(ck)
                if ck == KD + 4:
                    sp.wait_ge(s_xe, KD)
                    sp.dma_start(xdram.rearrange("p (k t) -> p k t", k=KD), xT[:, :, T:TT]).then_inc(s_xs, 16)
                i = ck - C_B - 6
                if 0 <= i < PADA:
                    if i >= 2:
                        sp.wait_ge(s_ac, i - 1)
                    e, k = divmod(i, KD)
                    sp.dma_start(aw[:, i % 2, :], wada[k, :, 2 * D + e * CW:2 * D + (e + 1) * CW]).then_inc(s_aw[i % 2], 16)
                if ck == C_WO:
                    sp.wait_ge(s_on, HEADS)
                    sp.wait_ge(s_xs, 16)
                    sp.dma_start(xres, xdram.rearrange("p (k t) -> p k t", k=KD)).then_inc(s_xb, 16)
            for i in range(4):
                sp.wait_ge(s_fe, i + 1)
                sp.wait_ge(s_feo, i + 1)
                half = slice(i % 2 * CW, (i % 2 + 1) * CW)
                sp.dma_start(orows[i // 2][:, half], outb[:, i // 2, half]).then_inc(s_out, 16)
            sp.wait_ge(s_out, 64)

        @block.gpsimd
        def _(pool):
            pool.wait_ge(s_at, 4)
            for e in range(8):
                if e:
                    pool.wait_ge(s_ap, e)
                for k in range(KD):
                    i = e * KD + k
                    if k == 0:
                        pool.memset(aacc[:, :], 0.0).then_inc(s_az, 1)
                        pool.wait_ge(s_az, e + 1)
                    else:
                        pool.wait_ge(s_ac, i)
                    pool.wait_ge(s_am, i + 1)
                    pool.tensor_tensor(aacc[:, :], aw[:, i % 2, :], aacc[:, :], ALU.add).then_inc(s_ac, 1)

        def halves(ap, h):
            v = ap.rearrange("p d (b n) -> p d b n", n=2 * h)
            return v[:, :, :, 0:h], v[:, :, :, h:2 * h]

        def abank(q, i):
            return (score[0:4, i, :] if q % 2 == 0 else (bank[2], ob)[i][0:4, :])

        def scaled(k):
            return zt[:, k // 2 % 2, k % 2, 0:T]

        @block.scalar
        def _(act):
            def hi(ck):
                act.wait_ge(s_raw[ck % RAW], 32 * (ck // RAW + 1))
                if ck >= SPL:
                    act.wait_ge(s_used, ck - SPL + 1)
                act.activation(whi[:, ck % SPL, :], raw[:, ck % RAW, :], ACT.Copy).then_inc(s_hi, 1)

            act.wait_ge(s_vec, 1)
            act.activation(cs[:, :, 0], vec[:, R_C:R_C + KD], ACT.Silu)
            act.activation(cs[:, :, 1], vec[:, R_CCTX:R_CCTX + KD], ACT.Silu).then_inc(s_cs, 1)
            act.preload_act_table_set(EXP_LN)
            act.wait_ge(s_cs, 1)
            act.wait_ge(s_lb, 1)
            act.activation(lbt[:, 1, :], lbt[:, 0, :], ACT.Exp).then_inc(s_lb, 1)
            act.activation(cs4[:, :, :, 0], cs[:, :, :], ACT.Copy).then_inc(s_c4, 1)

            def ada_product(i):
                act.wait_ge(s_aw[i % 2], 16 * (i // 2 + 1))
                act.activation(aw[:, i % 2, :], aw[:, i % 2, :], ACT.Copy,
                               scale=cs[:, i % KD, 0:1]).then_inc(s_am, 1)

            def mod_rows(q):
                act.wait_ge(s_used, KD * (q + 1))
                if q:
                    act.wait_ge(s_at, q)
                for i in range(2):
                    act.activation(arow[:, i * 512:(i + 1) * 512], abank(q, i), ACT.Copy).then_inc(s_ar, 1)

            for k in range(KD):
                hi(k)
                act.wait_ge(s_xe, k + 1)
                if k >= 2:
                    act.wait_ge(s_ms, k - 1)
                act.activation(sq[:, k % 2, :], xT[:, k, :], ACT.Square).then_inc(s_sq, 1)
            hi(KD)
            hi(KD + 1)
            act.wait_ge(s_ms, KD)
            act.activation(rstd[:, :], bank[3][:, :], ACT.Ln, bias=eps[:, :], scale=1.0 / D).then_inc(s_rs, 1)
            act.wait_ge(s_rs, 1)
            act.activation(rstd[:, :], rstd[:, :], ACT.Exp, scale=-0.5).then_inc(s_rs, 1)
            for ck in range(KD + 2, C_B):
                hi(ck)
                if ck % KD == 2:
                    mod_rows(ck // KD - 1)
            hi(C_B)
            mod_rows(3)
            act.wait_ge(s_mod, 6)
            act.wait_ge(s_xn, 2 * KD)
            for k in range(KD):
                for i, sh in enumerate((modc[:, 0, k:k + 1], mod[:, 0, k:k + 1])):
                    act.activation(ahi[:, k, i * T:(i + 1) * T], xT[:, k, i * T:(i + 1) * T], ACT.Identity,
                                   bias=sh).then_inc(s_ah, 1)
                if k % 2 == 1:
                    hi(C_B + k // 2 + 1)
                    if k >= 6:
                        ada_product(k // 2 - 3)
            ada_product(KD // 2 - 3)

            UNITS = ((0, 0), (1, 0), (0, 1), (1, 1))

            def gate_exps(pr, i):
                d, h = UNITS[i]
                b = pr % 2
                K = keyq[b][:, h, 2 * d, :]
                act.wait_ge(s_zc, 4 * pr + i + 1)
                if pr >= 2 and i == 0:
                    act.wait_ge(s_em, 2 * pr - 2)
                    act.wait_ge(s_sc, 4 * (2 * pr - 2))
                if 4 * pr + i >= 2:
                    act.wait_ge(s_zy, 2 * (4 * pr + i - 1))
                act.activation(K, gates[b][:, h, d, :], ACT.Exp, scale=-1.0).then_inc(s_ze, 1)
                act.wait_ge(s_ze, 3 * (4 * pr + i) + 1)
                act.activation(zt[:, i % 2, 0, :], K, ACT.Ln, bias=1.0).then_inc(s_ze, 1)
                act.activation(zt[:, i % 2, 1, :], K, ACT.Ln, bias=1.0,
                               scale=lbv[:, 2 * pr + h:2 * pr + h + 1]).then_inc(s_ze, 1)

            def gate_sigmoid(pr, i):
                d, h = UNITS[i]
                K = keyq[pr % 2][:, h, 2 * d, :]
                act.wait_ge(s_zy, 2 * (4 * pr + i) + 1)
                act.activation(K, K, ACT.Exp, scale=-1.0).then_inc(s_zk, 1)

            def queries(pr):
                b = pr % 2
                act.wait_ge(s_used, C_B + 16 * pr + 8)
                if pr >= 2:
                    act.wait_ge(s_sc, 4 * (2 * pr - 2))
                    act.wait_ge(s_xm, 2 * pr - 2)
                    act.wait_ge(s_em, 2 * pr - 2)
                act.activation(keyq[b][:, :, 1, T:TT], bank[2][:, :].rearrange("p (h t) -> p h t", h=2),
                               ACT.Silu).then_inc(s_qev, 1)
                act.preload_act_table_set(EXP_LN)

            def scan(j, n):
                m = n % 2
                if j == 4:
                    act.wait_ge(s_cum, n + 1)
                    if n:
                        act.wait_ge(s_tr, 2 * n)
                        act.wait_ge(s_o, n)
                        act.wait_ge(s_s2, n)
                    act.activation(xs[:, 0, 0, :], pcum[:, 0, 0:P], ACT.Exp, bias=tot[:, m, 0, 0:1], scale=-1.0)
                    act.activation(xs[:, 0, 1, :], pcum[:, 0, P:2 * P], ACT.Exp, bias=pcum[:, 0, 2 * P - 1:2 * P], scale=-1.0)
                    act.activation(xs[:, 0, 2, :], pcum[:, 0, 2 * P:3 * P], ACT.Exp, bias=pcum[:, 0, 3 * P - 1:3 * P], scale=-1.0)
                    act.activation(xs[:, 1, 0, :], pcum[:, 1, 0:P], ACT.Exp)
                    act.activation(xs[:, 1, 1, :], pcum[:, 1, P:2 * P], ACT.Exp, bias=tot[:, m, 1, 0:1])
                    act.activation(xs[:, 1, 2, :], pcum[:, 1, 3 * P:TT], ACT.Exp)
                    act.activation(xi[:, 0, :], pcum[:, 0, T:TT], ACT.Exp)
                    for t in range(2):
                        act.activation(xi[:, 1, t * P:(t + 1) * P], pcum[:, 1, T + t * P:T + (t + 1) * P], ACT.Exp,
                                       bias=tot[:, m, 1, 2 + t:3 + t], scale=-1.0)
                    act.activation(etot[:, m, 0:1], pcum[:, 0, 3 * P - 1:3 * P], ACT.Exp)
                    act.activation(etot[:, m, 1:2], tot[:, m, 1, 3:4], ACT.Exp).then_inc(s_ex, 1)
                if j == 2:
                    act.wait_ge(s_sub, 2 * n + 1)
                    act.activation(eseq[:, :, 0:3 * T], eseq[:, :, 0:3 * T], ACT.Exp).then_inc(s_el, 1)
                if j == 3:
                    act.wait_ge(s_sub, 2 * n + 2)
                    act.activation(eseq[:, :, 3 * T:NL * T], eseq[:, :, 3 * T:NL * T], ACT.Exp).then_inc(s_el, 1)
                if j == 7:
                    for d in range(2):
                        act.wait_ge(s_tr, 2 * n + d + 1)
                        act.activation(kt[:, d, :, :], (mx, ob)[d][:, 0:384].rearrange("p (j t) -> p j t", j=3),
                                       ACT.Copy).then_inc(s_kt, 1)
                if j == 8:
                    act.wait_ge(s_st, n + 1)
                    act.activation(state[:, 0, :, :], mx[:, 0:256].rearrange("p (d v) -> p d v", d=2),
                                   ACT.Copy).then_inc(s_s1, 1)
                if j == 10:
                    act.wait_ge(s_o, n + 1)
                    act.activation(osq, ob[:, 0:T], ACT.Square).then_inc(s_osq, 1)
                if j == 11:
                    act.wait_ge(s_om, n + 1)
                    if n:
                        act.wait_ge(s_on, n)
                    act.activation(rstd[:, 0:T], mx[:, 0:T], ACT.Ln, bias=eps[:, :], scale=1.0 / P).then_inc(s_ol, 1)
                    act.wait_ge(s_ol, n + 1)
                    act.activation(rstd[:, 0:T], rstd[:, 0:T], ACT.Exp, scale=-0.5).then_inc(s_or, 1)

            def gate_silu(u):
                act.wait_ge(s_used, C_G + 8 * (u + 1))
                for i in range(2):
                    if u:
                        act.wait_ge(s_y, 2 * u)
                    else:
                        act.wait_ge(s_zy, 8 * PAIRS)
                    act.activation(zt[:, i, 0, :], bank[2 * (u % 2) + i][:, :], ACT.Silu).then_inc(s_gev, 1)
                if u < 3:
                    act.preload_act_table_set(EXP_LN)

            for ck, kind, u, r, tasks in positions():
                if ck > C_B + KD // 2:
                    hi(ck)
                p = ck % 16
                z = C_B + 16 <= ck < C_G + 16
                if z and 1 <= p < 5:
                    gate_exps((ck - C_B) // 16 - 1, p - 1)
                if kind == "G" and r == 2 and u:
                    gate_silu(u - 1)
                for j, n in tasks:
                    scan(j, n)
                if z and 2 <= p < 6:
                    gate_sigmoid((ck - C_B) // 16 - 1, p - 2)
                if C_B + KD // 2 < ck <= C_B + PADA + 2:
                    ada_product(ck - C_B - 3)
                if kind == "Z" and r == 0:
                    queries(u)

            for k in range(KD):
                act.wait_ge(s_y, 2 * (k // 4) + (k % 4) // 2 + 1)
                if k >= 2:
                    act.wait_ge(s_used, C_WO + 2 * (k - 1))
                else:
                    act.wait_ge(s_used, C_WO - 7)
                act.activation(yhi[:, k % 2, :], oT[:, k, :], ACT.Copy).then_inc(s_yh, 1)
                hi(C_WO + 2 * k)
                if k == 0:
                    gate_silu(3)
                hi(C_WO + 2 * k + 1)
            act.preload_act_table_set(EXP_LN)
            hi(C_FF)
            for n, k in enumerate(LAST_BANK_FIRST):
                act.wait_ge(s_h, n + 1)
                if n >= 2:
                    act.wait_ge(s_hm, n - 1)
                act.activation(sq[:, n % 2, 0:T], hT[:, k, :], ACT.Square).then_inc(s_hq, 1)
            act.wait_ge(s_hm, KD)
            act.activation(rstd[:, 0:T], ob[:, 0:T], ACT.Ln, bias=eps[:, :], scale=1.0 / D).then_inc(s_hr, 1)
            act.wait_ge(s_hr, 1)
            act.activation(rstd[:, 0:T], rstd[:, 0:T], ACT.Exp, scale=-0.5).then_inc(s_hr, 1)
            act.wait_ge(s_av, 8)
            for k in range(KD):
                act.wait_ge(s_ht, k + 1)
                act.activation(ahi[:, k, 0:T], scaled(k), ACT.Identity, bias=mod[:, 3, k:k + 1]).then_inc(s_ah, 1)
                if k % 2 == 1:
                    hi(C_FF + k // 2 + 1)
            for u in range(2 * FG):
                for r in range(8):
                    ck = C_FF + 8 * u + r
                    if ck > C_FF + KD // 2:
                        hi(ck)
                    if r == 2 and u % 2 == 1:
                        j = u // 2
                        act.wait_ge(s_used, C_FF + 8 * u)
                        if j:
                            act.wait_ge(s_fh, 2 * j)
                        for i in range(2):
                            act.activation(sq[:, i, :], bank[i][:, :], ACT.Silu).then_inc(s_fgs, 1)
            for k in range(KF):
                act.wait_ge(s_fh, 2 * (k // 4) + (k % 4) // 2 + 1)
                if k >= 2:
                    act.wait_ge(s_used, C_DN + 2 * (k - 1))
                else:
                    act.wait_ge(s_used, C_FF)
                act.activation(yhi[:, k % 2, :], h1[:, k, :], ACT.Copy).then_inc(s_yh, 1)
                hi(C_DN + 2 * k)
                hi(C_DN + 2 * k + 1)
            act.preload_act_table_set(EXP_LN)
            for n, k in enumerate(SECOND_BANK_FIRST):
                act.wait_ge(s_fo, n + 1)
                if n >= 2:
                    act.wait_ge(s_fm, n - 1)
                act.activation(sq[:, n % 2, 0:T], hT[:, k, :], ACT.Square).then_inc(s_fq, 1)
            act.wait_ge(s_fm, KD)
            act.activation(fsum, bank[1][0:1, 0:T], ACT.Copy).then_inc(s_fe1, 1)
            act.wait_ge(s_fm, KD + 1)
            act.activation(rcol[:, 0, :], bank[1][:, T:T + 2], ACT.Ln, bias=eps[:, :], scale=1.0 / D).then_inc(s_fr, 1)
            act.wait_ge(s_fr, 1)
            act.activation(rcol[:, 1, :], rcol[:, 0, :], ACT.Exp, scale=-0.5).then_inc(s_fr, 1)
            act.wait_ge(s_fr, 2)
            for i in range(1, 8, 2):
                act.wait_ge(s_ft, i + 1)
                act.activation(outb[:, i // 4, (i % 4) * 512:(i % 4 + 1) * 512], all8[2 + i % 6], ACT.Copy,
                               scale=rcol[:, 1, i // 4:i // 4 + 1]).then_inc(s_feo, 1)

        def hidden(dve, j):
            dve.wait_ge(s_used, C_FF + 16 * (j + 1))
            for i in range(2):
                dve.wait_ge(s_fgs, 2 * j + i + 1)
                k = 4 * j + 2 * i
                dve.tensor_tensor(h1[:, k:k + 2, :], sq[:, i, :].rearrange("p (k t) -> p k t", k=2),
                                  bank[2 + i][:, :].rearrange("p (k t) -> p k t", k=2), ALU.mult).then_inc(s_fh, 1)

        @block.vector
        def _(dve):
            def lo(ck):
                dve.wait_ge(s_hi, ck + 1)
                dve.tensor_tensor(wlo[:, ck % SPL, :], raw[:, ck % RAW, :], whi[:, ck % SPL, :].bitcast(F32),
                                  ALU.subtract).then_inc(s_lo, 1)

            dve.memset(ones[:, :], 1.0)
            dve.memset(eps[:, :], EPS).then_inc(s_one, 1)
            dve.wait_ge(s_vecT, 1)
            dve.tensor_copy(vec[:, :], mx[:, 0:VROWS]).then_inc(s_vec, 1)
            dve.tensor_copy(bias[:, :], mx[:, 128:224]).then_inc(s_vec, 1)
            dve.wait_ge(s_vec, 2)
            lg = vec[:, R_LB:R_LB + KD]
            dve.tensor_tensor(lbt[:, 0, :], lg, lg, ALU.subtract).then_inc(s_lb, 1)
            dve.wait_ge(s_lb, 2)
            dve.reciprocal(lbt[:, 2, :], lbt[:, 1, :]).then_inc(s_lb, 1)
            dve.wait_ge(s_lb, 3)
            dve.tensor_tensor(lbt[:, 0, :], lbt[:, 1, :], lbt[:, 2, :], ALU.mult).then_inc(s_lb, 1)
            dve.wait_ge(s_lb, 4)
            dve.tensor_tensor(lbv, lbt[:, 0, :], lbt[:, 0, :], ALU.subtract).then_inc(s_lb, 1)
            dve.wait_ge(s_lb, 5)
            dve.tensor_scalar(oml[:, :], lbv, -1.0, 1.0, ALU.mult, ALU.add).then_inc(s_mod, 1)
            dve.wait_ge(s_c4, 1)
            dve.tensor_tensor(cs4[:, :, :, 1], cs[:, :, :], cs4[:, :, :, 0].bitcast(F32), ALU.subtract).then_inc(s_c4, 1)
            for k in range(KD):
                if k:
                    lo(k - 1)
                dve.wait_ge(s_xt, k + 1)
                dve.tensor_copy(xT[:, k, :], bank[k % 2][:, :]).then_inc(s_xe, 1)
            am = mx[:, 0:128].rearrange("p (m k s i) -> p m k s i", m=2, s=2, i=2)

            def modulation(i, m, c):
                b = bias[:, m * KD:(m + 1) * KD]
                dve.wait_ge(s_at, 2 * (i + 1))
                dve.tensor_tensor(mod[:, m, :], am[:, i, :, 0, 0], b, ALU.add)
                dve.tensor_tensor(modc[:, m, :], am[:, i, :, 1, 0], b, ALU.add).then_inc(s_mod, 1)
                dve.wait_ge(s_mod, c)
                dve.tensor_tensor(mod[:, m, :], am[:, i, :, 0, 1], mod[:, m, :], ALU.add)
                dve.tensor_tensor(modc[:, m, :], am[:, i, :, 1, 1], modc[:, m, :], ALU.add).then_inc(s_mod, 1)

            for ck in range(KD - 1, C_B):
                lo(ck)
                if ck == 2 * KD + 3:
                    modulation(0, 1, 2)
                    dve.wait_ge(s_mod, 3)
                    nm = vec[:, R_NMIX:R_NMIX + KD]
                    dve.scalar_tensor_tensor(out=scl[:, 0, :], in0=modc[:, 1, :], scalar=1.0, in1=nm, op0=ALU.add,
                                             op1=ALU.mult)
                    dve.scalar_tensor_tensor(out=scl[:, 1, :], in0=mod[:, 1, :], scalar=1.0, in1=nm, op0=ALU.add,
                                             op1=ALU.mult).then_inc(s_mod, 1)
                k = ck - 2 * KD - 5
                if 0 <= k < KD:
                    if k == 0:
                        dve.wait_ge(s_rs, 2)
                        dve.wait_ge(s_mod, 4)
                        dve.wait_ge(s_xs, 16)
                    for i in range(2):
                        v = xT[:, k, i * T:(i + 1) * T]
                        dve.scalar_tensor_tensor(out=v, in0=v, scalar=scl[:, i, k:k + 1], in1=rstd[:, i * T:(i + 1) * T],
                                                 op0=ALU.mult, op1=ALU.mult).then_inc(s_xn, 1)
            lo(C_B)
            modulation(1, 0, 5)
            dve.wait_ge(s_mod, 6)
            dve.wait_ge(s_xn, 2 * KD)

            def a_lo(k):
                for i, sh in enumerate((modc[:, 0, k:k + 1], mod[:, 0, k:k + 1])):
                    h = slice(i * T, (i + 1) * T)
                    dve.wait_ge(s_ah, 2 * k + i + 1)
                    dve.scalar_tensor_tensor(out=alo[:, k, h], in0=xT[:, k, h], scalar=sh,
                                             in1=ahi[:, k, h].bitcast(F32), op0=ALU.add,
                                             op1=ALU.subtract).then_inc(s_al, 1)

            for k in range(KD):
                if k:
                    a_lo(k - 1)
                if k % 2 == 0 and k:
                    lo(C_B + k // 2)
            a_lo(KD - 1)
            lo(C_B + KD // 2)

            UNITS = ((0, 0), (1, 0), (0, 1), (1, 1))

            def clip_gates(pr):
                dve.wait_ge(s_used, C_B + 16 * (pr + 1))
                if pr >= 2:
                    dve.wait_ge(s_cum, 2 * pr - 2)
                for i, (d, h) in enumerate(UNITS):
                    dve.tensor_scalar(gates[pr % 2][:, h, d, :], bank[2 * d + h][:, :], -CLIP, CLIP, ALU.max,
                                      ALU.min).then_inc(s_zc, 1)

            def log_gates(pr, i):
                d, h = UNITS[i]
                b = pr % 2
                n = 4 * pr + i
                G, K = gates[b][:, h, d, :], keyq[b][:, h, 2 * d, :]
                dve.wait_ge(s_ze, 3 * n + 3)
                dve.wait_ge(s_zc, n + 1)
                dve.tensor_tensor(K, G, zt[:, i % 2, 0, :], ALU.add).then_inc(s_zy, 1)
                dve.wait_ge(s_zy, 2 * n + 1)
                dve.tensor_tensor(G, zt[:, i % 2, 1, :], zt[:, i % 2, 0, :], ALU.subtract).then_inc(s_zy, 1)

            def keys(pr, i):
                d, h = UNITS[i]
                K = keyq[pr % 2][:, h, 2 * d, :]
                dve.wait_ge(s_zk, 4 * pr + i + 1)
                dve.tensor_scalar(K, K, oml[:, 2 * pr + h:2 * pr + h + 1], None, ALU.mult).then_inc(s_k, 1)

            def values(pr):
                dve.wait_ge(s_used, C_B + 16 * pr + 8)
                if pr >= 2:
                    dve.wait_ge(s_o, 2 * pr - 2)
                for i in range(2):
                    dve.tensor_copy(vals[pr % 2][:, 2 * i:2 * i + 2, :],
                                    bank[i][:, :].rearrange("p (t v) -> p t v", t=2)).then_inc(s_vev, 1)

            def scale_queries(pr):
                dve.wait_ge(s_qev, pr + 1)
                Q = keyq[pr % 2][:, :, 1, T:TT]
                dve.tensor_scalar(Q, Q, QSCALE, None, ALU.mult).then_inc(s_qs, 1)

            def levels(n, which):
                for li in which:
                    h = HALVES[li]
                    xl, xr = halves(pcum[:, :, T:TT], h)
                    el, er = halves(ebuf[:, :, li, :], h)
                    nb = T // (2 * h)
                    r = mid_ap(h, nb)
                    dve.tensor_tensor(el, r, xl, ALU.subtract)
                    last = dve.tensor_tensor(er, xr, r, ALU.subtract)
                last.then_inc(s_sub, 1)

            def mid_ap(h, nb):
                full = pcum[:, :, T:TT]
                pstep = full.ap[0]
                return bass.AP(tensor=full.tensor, offset=full.offset + h - 1,
                               ap=[list(pstep), [TT + 1, 2], [2 * h, nb], [0, h]])

            def level_muls(n, which, last_one):
                b, hh = (n // 2) % 2, n % 2
                kq = keyq[b][:, hh, :, T:TT]
                for li in which:
                    h = HALVES[li]
                    el, er = halves(ebuf[:, :, li, :], h)
                    ml, _ = halves(kq[:, 0:2, :], h)
                    _, mr = halves(kq[:, 1:3, :], h)
                    dve.tensor_tensor(el, el, ml, ALU.mult)
                    last = dve.tensor_tensor(er, er, mr, ALU.mult)
                if last_one:
                    last.then_inc(s_em, 1)

            def place(n, step):
                d, t = divmod(step, 2)
                dve.wait_ge(s_sc, 4 * n + step + 1)
                if d == 0:
                    dve.tensor_tensor(pT[:, t, :], score[:, 1, 3 * P:4 * P], ident[:, :], ALU.mult).then_inc(s_dg, 1)
                    dve.wait_ge(s_dg, 2 * n + t + 1)
                for li, h in enumerate(HALVES):
                    h0 = h if d == 0 else 0
                    dst = pT[:, t, :].rearrange("p (b n) -> p b n", n=2 * h)[:, :, h0:h0 + h]
                    src = score[:, li // 4, (li % 4) * P:(li % 4 + 1) * P]
                    src = src.rearrange("p (b n) -> p b n", n=2 * h)[:, :, h0:h0 + h]
                    off = (d * NL + li) * 64
                    m = masks[:, off:off + 64].rearrange("p (b n) -> p b n", n=h)
                    dve.copy_predicated(dst, m, src).then_inc(s_pl, 1)
                    dve.wait_ge(s_pl, (4 * n + step) * NL + li + 1)

            def scan(j, n):
                b, hh, m = (n // 2) % 2, n % 2, n % 2
                G, KQ = gates[b], keyq[b]
                if j == 0:
                    dve.wait_ge(s_k, 4 * (n // 2) + 2 * hh + 2)
                    dve.wait_ge(s_zy, 2 * (4 * (n // 2) + 2 * hh + 2))
                    dve.wait_ge(s_qs, n // 2 + 1)
                    if n:
                        dve.wait_ge(s_ex, n)
                        dve.wait_ge(s_sub, 2 * n)
                    if n >= 2:
                        dve.wait_ge(s_s2, n - 1)
                    dve.tensor_tensor_scan(pcum[:, 0, :], keep[:, :], G[:, hh, 0, :], 0.0, ALU.mult, ALU.add)
                    g1 = G[:, hh, 1, :]
                    shifted = bass.AP(tensor=g1.tensor, offset=g1.offset - 1, ap=[list(a) for a in g1.ap])
                    dve.tensor_tensor_scan(pcum[:, 1, :], shifted, keep[:, :], 0.0, ALU.add, ALU.mult).then_inc(s_cd, 1)
                    dve.wait_ge(s_cd, n + 1)
                    dve.tensor_tensor(tot[:, m, 0, 0:1], pcum[:, 0, P - 1:P], pcum[:, 0, 2 * P - 1:2 * P], ALU.add)
                    ends = slice(P - 1, TT, P)
                    dve.tensor_tensor(tot[:, m, 1, 0:4], pcum[:, 1, ends], G[:, hh, 1, ends], ALU.add).then_inc(s_cum, 1)
                    if n:
                        dve.wait_ge(s_sc, 4 * n - 2)
                    dve.tensor_tensor(ksum, KQ[:, hh, 0, T:TT], KQ[:, hh, 2, T:TT], ALU.add)
                if j == 9:
                    place(n, 3)
                if j == 1:
                    if n:
                        dve.wait_ge(s_sc, 4 * n)
                    levels(n, (0, 1, 2))
                if j == 2:
                    levels(n, (3, 4, 5, 6))
                if j == 5:
                    dve.wait_ge(s_ex, n + 1)
                    dve.tensor_tensor(xs[:, 0, :, :], xs[:, 0, :, :],
                                      KQ[:, hh, 0, 0:3 * P].rearrange("p (j t) -> p j t", j=3), ALU.mult)
                    dve.tensor_tensor(xs[:, 1, 0:2, :], xs[:, 1, 0:2, :],
                                      KQ[:, hh, 2, 0:2 * P].rearrange("p (j t) -> p j t", j=2), ALU.mult)
                    dve.tensor_tensor(xs[:, 1, 2, :], xs[:, 1, 2, :], KQ[:, hh, 2, 3 * P:TT], ALU.mult)
                    for d in range(2):
                        last = dve.tensor_tensor(xi[:, d, :], xi[:, d, :], KQ[:, hh, 1, T:TT], ALU.mult)
                    last.then_inc(s_xm, 1)
                if j == 3:
                    dve.wait_ge(s_el, 2 * n + 1)
                    level_muls(n, (0, 1, 2), False)
                if j == 4:
                    dve.wait_ge(s_el, 2 * n + 2)
                    level_muls(n, (3, 4, 5, 6), True)
                if 6 <= j <= 8:
                    if j == 6 and n:
                        dve.wait_ge(s_o, n)
                    place(n, j - 6)
                if j == 8:
                    dve.wait_ge(s_s1, n + 1)
                    for d in range(2):
                        last = dve.scalar_tensor_tensor(out=state[:, 1, d, :], in0=state[:, 0, d, :],
                                                        scalar=etot[:, m, d:d + 1],
                                                        in1=mx[:, 256 + d * P:384 + d * P], op0=ALU.mult, op1=ALU.add)
                    last.then_inc(s_s2, 1)
                if j == 12:
                    dve.wait_ge(s_or, n + 1)
                    dve.scalar_tensor_tensor(out=oT[:, n, :], in0=ob[:, 0:T], scalar=vec[:, R_ONORM:R_ONORM + 1],
                                             in1=rstd[:, 0:T], op0=ALU.mult, op1=ALU.mult).then_inc(s_on, 1)

            def gate_outputs(u):
                for i in range(2):
                    dve.wait_ge(s_gev, 2 * u + i + 1)
                    dve.wait_ge(s_on, 4 * u + 2 * i + 2)
                    v = oT[:, 4 * u + 2 * i:4 * u + 2 * i + 2, :]
                    dve.tensor_tensor(v, v, zt[:, i, 0, :].rearrange("p (k t) -> p k t", k=2), ALU.mult).then_inc(s_y, 1)

            def add_modulation(e):
                dve.wait_ge(s_ap, e + 1)
                v = mod[:, 2 + e // 2, (e % 2) * 8:(e % 2) * 8 + 8]
                o = 2 * KD + 8 * e
                dve.tensor_tensor(v, bank[3][:, 0:8], bias[:, o:o + 8], ALU.add).then_inc(s_av, 1)

            for ck, kind, u, r, tasks in positions():
                if ck > C_B + KD // 2:
                    lo(ck)
                if kind == "Z" and r == 1:
                    scale_queries(u)
                p = ck % 16
                if 2 <= p < 7 and C_B + 16 <= ck < C_G + 7:
                    pr = (ck - C_B) // 16 - 1
                    if p <= 5:
                        log_gates(pr, p - 2)
                    if p >= 3:
                        keys(pr, p - 3)
                if kind == "G" and r == 3 and u:
                    gate_outputs(u - 1)
                if ada_at(ck) is not None:
                    add_modulation(ada_at(ck))
                for j, n in tasks:
                    scan(j, n)
                if kind == "Z" and r == 0:
                    values(u)
                if p == 0 and C_B + 16 <= ck <= C_G:
                    clip_gates((ck - C_B) // 16 - 1)

            for k in range(KD):
                if k == 1:
                    gate_outputs(3)
                dve.wait_ge(s_yh, k + 1)
                dve.wait_ge(s_y, 2 * (k // 4) + (k % 4) // 2 + 1)
                dve.tensor_tensor(ylo[:, k % 2, :], oT[:, k, :], yhi[:, k % 2, :].bitcast(F32), ALU.subtract).then_inc(s_yl, 1)
                lo(C_WO + 2 * k)
                lo(C_WO + 2 * k + 1)
            dve.wait_ge(s_av, 8)
            dve.scalar_tensor_tensor(out=sclf[:, :], in0=mod[:, 4, :], scalar=1.0, in1=vec[:, R_NFFN:R_NFFN + KD],
                                     op0=ALU.add, op1=ALU.mult).then_inc(s_mod, 1)
            dve.wait_ge(s_used, C_FF)
            dve.wait_ge(s_xb, 16)
            for k in LAST_BANK_FIRST:
                dve.scalar_tensor_tensor(out=hT[:, k, :], in0=all8[k // 2][:, (k % 2) * T:(k % 2) * T + T],
                                         scalar=mod[:, 2, k:k + 1], in1=xres[:, k, :], op0=ALU.mult,
                                         op1=ALU.add).then_inc(s_h, 1)
            lo(C_FF)
            dve.wait_ge(s_hr, 2)
            dve.wait_ge(s_mod, 7)
            dve.wait_ge(s_h, KD)

            def f_lo(k):
                dve.wait_ge(s_ah, 2 * KD + k + 1)
                dve.scalar_tensor_tensor(out=alo[:, k, 0:T], in0=scaled(k), scalar=mod[:, 3, k:k + 1],
                                         in1=ahi[:, k, 0:T].bitcast(F32), op0=ALU.add, op1=ALU.subtract).then_inc(s_al, 1)

            def scale_h(k):
                if k >= 4:
                    dve.wait_ge(s_al, 2 * KD + k - 3)
                dve.scalar_tensor_tensor(out=scaled(k), in0=hT[:, k, :], scalar=sclf[:, k:k + 1], in1=rstd[:, 0:T],
                                         op0=ALU.mult, op1=ALU.mult).then_inc(s_ht, 1)

            scale_h(0)
            scale_h(1)
            for k in range(KD):
                if k + 2 < KD:
                    scale_h(k + 2)
                f_lo(k)
                if k % 2 == 1:
                    lo(C_FF + k // 2 + 1)
            for u in range(2 * FG):
                for r in range(8):
                    ck = C_FF + 8 * u + r
                    if ck > C_FF + KD // 2:
                        lo(ck)
                    if r == 2 and u % 2 == 0 and u:
                        hidden(dve, u // 2 - 1)
            for k in range(KF):
                if k == 1:
                    hidden(dve, FG - 1)
                dve.wait_ge(s_yh, KD + k + 1)
                dve.wait_ge(s_fh, 2 * (k // 4) + (k % 4) // 2 + 1)
                dve.tensor_tensor(ylo[:, k % 2, :], h1[:, k, :], yhi[:, k % 2, :].bitcast(F32), ALU.subtract).then_inc(s_yl, 1)
                lo(C_DN + 2 * k)
                lo(C_DN + 2 * k + 1)
            dve.wait_ge(s_used, CHUNKS)
            for k in SECOND_BANK_FIRST:
                dve.scalar_tensor_tensor(out=hT[:, k, :], in0=all8[k // 2][:, (k % 2) * T:(k % 2) * T + T],
                                         scalar=mod[:, 5, k:k + 1], in1=hT[:, k, :], op0=ALU.mult,
                                         op1=ALU.add).then_inc(s_fo, 1)
            for n, k in enumerate(SECOND_BANK_FIRST):
                dve.wait_ge(s_fq, n + 1)
                dve.wait_ge(s_fo, n + 1)
                dve.tensor_scalar(hT[:, k, :], hT[:, k, :], vec[:, R_FIN + k:R_FIN + k + 1], None,
                                  ALU.mult).then_inc(s_fs, 1)
            dve.wait_ge(s_fr, 2)
            for i in range(0, 8, 2):
                dve.wait_ge(s_ft, i + 1)
                dve.tensor_scalar(outb[:, i // 4, (i % 4) * 512:(i % 4 + 1) * 512], all8[2 + i % 6],
                                  rcol[:, 1, i // 4:i // 4 + 1], None, ALU.mult).then_inc(s_fe, 1)

        def mean_square(pe, k):
            pe.wait_ge(s_one, 1)
            pe.wait_ge(s_sq, k + 1)
            pe.matmul(bank[3][:, :], ones[:, :], sq[:, k % 2, :], start=(k == 0), stop=(k == KD - 1)).then_inc(s_ms, 1)

        def mod_sum(pe, ck):
            q, k = divmod(ck, KD)
            pe.wait_ge(s_lo, ck + 1)
            if ck == 0:
                pe.wait_ge(s_c4, 2)
            if q >= 2 and k == 0:
                pe.wait_ge(s_ar, 2 * (q - 1))
            cc = cs4[:, k, :, :].rearrange("p s i -> p (s i)")
            for i in range(2):
                pe.matmul(abank(q, i), cc, whi[:, ck % SPL, i * 512:(i + 1) * 512], start=(k == 0), stop=False)
                last = pe.matmul(abank(q, i), cc, wlo[:, ck % SPL, i * 512:(i + 1) * 512], start=False, stop=(k == KD - 1))
            last.then_inc(s_used, 1)

        def turn_rows(pe, q):
            pe.wait_ge(s_ar, 2 * (q + 1))
            if q == 0:
                pe.wait_ge(s_vec, 2)
            for f in range(8):
                o = 32 * q + 4 * f
                last = pe.transpose(mx[:, o:o + 4], arow[:, f * P:(f + 1) * P], ident[0:4, 0:4])
            last.then_inc(s_at, 1)

        @block.tensor
        def _(pe):
            pe.wait_ge(s_const, 16 * 11)
            pe.transpose(mx[:, 0:VROWS], vrow[0:VROWS, :], ident[0:VROWS, 0:VROWS])
            pe.transpose(mx[:, 128:224], brow[0:96, :], ident[0:96, 0:96]).then_inc(s_vecT, 1)
            for t in range(4):
                pe.wait_ge(s_x[t], 16)
            def turn_x(k):
                if k >= 2:
                    pe.wait_ge(s_xe, k - 1)
                for t in range(4):
                    last = pe.transpose(bank[k % 2][:, t * P:(t + 1) * P], xin[:, t, k * P:(k + 1) * P], ident[:, :])
                last.then_inc(s_xt, 1)

            turn_x(0)
            for k in range(KD):
                if k + 1 < KD:
                    turn_x(k + 1)
                if k >= 1:
                    mean_square(pe, k - 1)
                mod_sum(pe, k)
            mean_square(pe, KD - 1)
            for i in range(KD, C_B):
                mod_sum(pe, i)
                if i % KD == 1 and i > KD:
                    turn_rows(pe, i // KD - 1)
            turn_rows(pe, 3)

            def three(dst, w, wl, ah, al, start, stop):
                pe.matmul(dst, w, ah, start=start, stop=False, skip_group_check=True)
                pe.matmul(dst, w, al, start=False, stop=False, skip_group_check=True)
                return pe.matmul(dst, wl, ah, start=False, stop=stop, skip_group_check=True)

            def chunk(ck, kind, r, u=0, between=()):
                s = ck % SPL
                for a in range(2):
                    if a:
                        for j, n in between:
                            scan(j, n)
                        if sum_at(ck) is not None:
                            sum_modulation(sum_at(ck))
                    k = 2 * r + a
                    first, end = k == 0, k == KD - 1
                    if ck < C_B + 8 and kind == "VQ":
                        pe.wait_ge(s_al, 2 * (k + 1))
                    if kind == "FF" and u == 0:
                        pe.wait_ge(s_al, 2 * KD + k + 1)
                    if kind == "VQ":
                        for t in (0, 1, None, 2, 3):
                            if t is None:
                                if first and u:
                                    pe.wait_ge(s_zc, 4 * (u - 1) + 2)
                                for f in range(2):
                                    o = slice(512 * a + 256 + f * P, 512 * a + 256 + (f + 1) * P)
                                    three(bank[2][:, f * T:(f + 1) * T], whi[:, s, o], wlo[:, s, o],
                                          ahi[:, k, T:TT], alo[:, k, T:TT], first and f == 0, end)
                                continue
                            if first and u and t % 2 == 0:
                                pe.wait_ge(s_zc, 4 * (u - 1) + 1 + t)
                            dst = bank[t // 2][:, (t % 2) * T:(t % 2 + 1) * T]
                            o = slice(512 * a, 512 * a + 256)
                            tk = slice(t * P, (t + 1) * P)
                            st = first and t % 2 == 0
                            pe.matmul(dst, ahi[:, k, tk], whi[:, s, o], start=st, stop=False, skip_group_check=True)
                            pe.matmul(dst, ahi[:, k, tk], wlo[:, s, o], start=False, stop=False, skip_group_check=True)
                            last = pe.matmul(dst, alo[:, k, tk], whi[:, s, o], start=False, stop=end, skip_group_check=True)
                    elif kind == "Z":
                        for f in (3, 0, 1, 2):
                            if first and f == 3:
                                if u:
                                    pe.wait_ge(s_zc, 4 * u)
                                    pe.wait_ge(s_av, u)
                            if first and f < 2:
                                pe.wait_ge(s_vev, 2 * u + f + 1)
                            if first and f == 2:
                                pe.wait_ge(s_qev, u + 1)
                            o = slice(512 * a + f * P, 512 * a + (f + 1) * P)
                            last = three(bank[f][:, :], whi[:, s, o], wlo[:, s, o], ahi[:, k, :], alo[:, k, :], first, end)
                    else:
                        tk = slice(T, TT) if kind == "G" else slice(0, T)
                        bb = 2 * (u % 2)
                        for f in range(4):
                            if kind == "G" and u == 0 and first and f % 2 == 0:
                                pe.wait_ge(s_zc, 4 * (PAIRS - 1) + 1 + f)
                            o = slice(512 * a + f * P, 512 * a + (f + 1) * P)
                            last = three(bank[bb + f // 2][:, (f % 2) * T:(f % 2 + 1) * T], whi[:, s, o], wlo[:, s, o],
                                         ahi[:, k, tk], alo[:, k, tk], first and f % 2 == 0, end)
                last.then_inc(s_used, 1)

            def wide(ck, i, half, k_end, frees):
                s = ck % SPL
                for f in range(8):
                    ft = 8 * half + f
                    if i == 0 and ft in frees:
                        pe.wait_ge(*frees[ft])
                    o = slice(f * P, (f + 1) * P)
                    last = three(all8[ft // 2][:, (ft % 2) * T:(ft % 2 + 1) * T], whi[:, s, o], wlo[:, s, o],
                                 yhi[:, i % 2, :], ylo[:, i % 2, :], i == 0 and ft % 2 == 0, i == k_end)
                last.then_inc(s_used, 1)

            def scan(j, n):
                b, hh = (n // 2) % 2, n % 2
                KQ = keyq[b]
                V = vals[b][:, :, hh * P:(hh + 1) * P]
                if j == 6:
                    pe.wait_ge(s_xm, n + 1)
                    for d in range(2):
                        if n:
                            pe.wait_ge(s_on, n)
                        for i in range(3):
                            last = pe.transpose((mx, ob)[d][:, i * P:(i + 1) * P], xs[:, d, i, :], ident[:, :])
                        last.then_inc(s_tr, 1)
                if j == 7:
                    pe.wait_ge(s_kt, 2 * n + 2)
                    pe.wait_ge(s_vev, 2 * (n // 2) + 2)
                    for d in range(2):
                        for t in range(2):
                            pe.matmul(mx[:, d * P:(d + 1) * P], kt[:, d, t, :], V[:, t, :], start=(t == 0), stop=(t == 1))
                    for d in range(2):
                        last = pe.matmul(mx[:, 256 + d * P:384 + d * P], kt[:, d, 2, :], V[:, 2 + d, :], start=True, stop=True)
                    last.then_inc(s_st, 1)
                if 5 <= j <= 8:
                    d, t = divmod(j - 5, 2)
                    pe.wait_ge(s_em, n + 1)
                    if n or j > 5:
                        pe.wait_ge(s_pl, (4 * n + j - 5) * NL)
                    for li in range(NL):
                        e = ebuf[:, d, li, t * P:(t + 1) * P]
                        last = pe.matmul(score[:, li // 4, (li % 4) * P:(li % 4 + 1) * P], e, e, start=True, stop=True)
                    if d == 0:
                        last = pe.matmul(score[:, 1, 3 * P:4 * P], ksum[:, t * P:(t + 1) * P],
                                         KQ[:, hh, 1, T + t * P:T + (t + 1) * P], start=True, stop=True)
                    last.then_inc(s_sc, 1)
                if j == 9:
                    pe.wait_ge(s_pl, (4 * n + 4) * NL)
                    pe.wait_ge(s_s2, n + 1)
                    for t in range(2):
                        o = ob[:, t * P:(t + 1) * P]
                        pe.matmul(o, V[:, 2 + t, :], pT[:, t, :], start=True, stop=False)
                        pe.matmul(o, state[:, t, 0, :], xi[:, 0, t * P:(t + 1) * P], start=False, stop=False)
                        last = pe.matmul(o, state[:, 1 - t, 1, :], xi[:, 1, t * P:(t + 1) * P], start=False, stop=True)
                    last.then_inc(s_o, 1)
                if j == 10:
                    pe.wait_ge(s_osq, n + 1)
                    pe.matmul(mx[:, 0:T], ones[:, :], osq, start=True, stop=True).then_inc(s_om, 1)

            def sum_modulation(e):
                pe.wait_ge(s_ac, KD * (e + 1))
                pe.wait_ge(s_zc, 4 * (e + 1))
                for f in range(8):
                    last = pe.matmul(bank[3][:, f:f + 1], aacc[:, f * P:(f + 1) * P], ones[:, 0:1], start=True, stop=True)
                last.then_inc(s_ap, 1)

            for ck, kind, u, r, tasks in positions():
                if kind == "G" and r == 0:
                    if u == 1:
                        pe.wait_ge(s_zc, 4 * PAIRS)
                    elif u >= 2:
                        pe.wait_ge(s_gev, 2 * (u - 1))
                    if u == 1:
                        pe.wait_ge(s_av, 8)
                pe.wait_ge(s_lo, ck + 1)
                chunk(ck, kind, r, u, tasks)
            for k in range(KD):
                pe.wait_ge(s_yl, k + 1)
                for half in range(2):
                    ck = C_WO + 2 * k + half
                    pe.wait_ge(s_lo, ck + 1)
                    wide(ck, k, half, KD - 1, {0: (s_gev, 6), 4: (s_gev, 7), 6: (s_gev, 8), 8: (s_on, HEADS)})
            for k in range(KD):
                pe.wait_ge(s_hq, k + 1)
                if k == 0:
                    pe.wait_ge(s_h, 2)
                pe.matmul(ob[:, 0:T], ones[:, :], sq[:, k % 2, 0:T], start=(k == 0), stop=(k == KD - 1)).then_inc(s_hm, 1)
            for u in range(2 * FG):
                j = u // 2
                if j:
                    if u % 2 == 0:
                        pe.wait_ge(s_fgs, 2 * j)
                    else:
                        pe.wait_ge(s_fh, 2 * j)
                for r in range(8):
                    ck = C_FF + 8 * u + r
                    pe.wait_ge(s_lo, ck + 1)
                    chunk(ck, "FF", r, u)
            for k in range(KF):
                pe.wait_ge(s_yl, KD + k + 1)
                for half in range(2):
                    ck = C_DN + 2 * k + half
                    pe.wait_ge(s_lo, ck + 1)
                    wide(ck, k, half, KF - 1, {0: (s_fgs, 2 * FG), 4: (s_fh, 2 * FG - 1), 6: (s_fh, 2 * FG), 8: (s_hr, 1)})
            for k in range(KD):
                pe.wait_ge(s_fq, k + 1)
                if k == 0:
                    pe.wait_ge(s_fo, 2)
                pe.matmul(bank[1][0:1, 0:T], ones[:, 0:1], sq[:, k % 2, 0:T], start=(k == 0),
                          stop=(k == KD - 1)).then_inc(s_fm, 1)
            pe.wait_ge(s_fe1, 1)
            for t in range(2):
                last = pe.transpose(bank[1][:, T + t:T + t + 1], fsum[:, t * P:(t + 1) * P], ident[0:1, 0:1])
            last.then_inc(s_fm, 1)
            pe.wait_ge(s_fo, KD)
            for t in range(2):
                for q in range(4):
                    i = 4 * t + q
                    if i >= 6:
                        pe.wait_ge(s_fe if i % 2 == 0 else s_feo, 1)
                    pe.wait_ge(s_fs, 4 * (q + 1))
                    for f in range(4):
                        k = 4 * q + f
                        last = pe.transpose(all8[2 + i % 6][:, f * P:(f + 1) * P], hT[:, k, t * P:(t + 1) * P], ident[:, :])
                    last.then_inc(s_ft, 1)

def sum_at(ck):
    e, p = divmod(ck - C_B, 16)
    return e - 1 if p == 2 and 1 <= e <= 8 and ck < C_G + 16 else None


def ada_at(ck):
    e, p = divmod(ck - C_B, 16)
    return e - 1 if p == 3 and 1 <= e <= 8 and ck < C_G + 16 else None


LAST_BANK_FIRST = [14, 15] + list(range(14))
SECOND_BANK_FIRST = [2, 3, 0, 1] + list(range(4, KD))


def shape_constants():
    ident = np.eye(P, dtype=np.float32)
    keep = np.ones((P, TT), np.float32)
    keep[:, ::P] = 0.0
    masks = np.zeros((P, 2, NL, 64), np.uint32)
    s = np.arange(P)[:, None]
    j = np.arange(64)[None, :]
    for li, h in enumerate(HALVES):
        for d in range(2):
            t = (j // h) * 2 * h + j % h + (h if d == 0 else 0)
            same = s // (2 * h) == t // (2 * h)
            left = s % (2 * h) < h
            masks[:, d, li, :] = same & (left if d == 0 else ~left)
    return ident, keep, masks.reshape(P, 2 * NL * 64)


_INS = ["x", "c", "ctx", "c_ctx", "w_ada", "b_ada", "norm_mix", "norm_ffn", "hg_lb_logits", "hg_w_in", "hg_w_f",
        "hg_o_norm", "hg_w_o", "ffn_w_gate", "ffn_w_up", "ffn_w_down", "final_norm"]


def kernel(**inputs):
    import numpy as _np
    import concourse.bacc as _bacc
    from concourse import mybir as _mybir
    from concourse.bass_utils import run_bass_kernel_spmd as _run

    nc = _bacc.Bacc("TRN2", target_bir_lowering=False, num_devices=1, dynamic_dma_scratch_size=1024)
    arrays, args = {}, []
    ident, keep, masks = shape_constants()
    named = [(n, _np.ascontiguousarray(inputs[n])) for n in _INS]
    named += [("ident", ident), ("keep", keep), ("masks", masks)]
    for name, a in named:
        arrays[f"in_{name}_dram"] = a
        args.append(nc.dram_tensor(f"in_{name}_dram", a.shape, _mybir.dt.from_np(a.dtype), kind="ExternalInput").ap())
    args.append(nc.dram_tensor("out_0_dram", (1, T, D), _mybir.dt.float32, kind="ExternalOutput").ap())
    build(nc, *args)
    r = _run(nc, [arrays], core_ids=[0])
    return r.results[0]["out_0_dram"]
```
